# Optimizing a Trainium2 kernel written in Bass

```python
import math
import jax, jax.numpy as jnp
from jax import lax
import numpy as np

D_MODEL = 1024
BATCH = 1
SEQ = 2048
DEPTH = 1
DEC_BATCH = 1
DEC_SEQ = 32
PAST_LEN = 512

CHUNK = 64
D_HEAD = 64
H_A = 4
H_B = 4
H_C = 4
DK_C = 128
DV_C = 128
W_A = H_A * D_HEAD
W_B = H_B * D_HEAD
QK_C = H_C * DK_C
W_C = H_C * DV_C
D_MIX = W_A + W_B + W_C
N_PREV_CHUNKS = 8
BAND = N_PREV_CHUNKS + 1
REL_CLIP = 128
N_REL = 2 * REL_CLIP + 1
D_FF = 4 * D_MODEL
Q_BLOCK = 128
EPS = 1e-6
NEG_BIG = -1e30
LB_FLOOR = 1e-30
_SIZES = [W_A, W_A, W_A, W_B, W_B, W_B, QK_C, QK_C, W_C, W_C]
D_IN = sum(_SIZES)
SPLITS = [int(s) for s in np.cumsum(_SIZES)[:-1]]

kernel_name = "hymba_style_sb_band_hgrn2_encoder_step"

def rmsnorm(x, g):
    xf = x.astype(jnp.float32)
    y = xf * lax.rsqrt(jnp.mean(xf * xf, axis=-1, keepdims=True) + EPS)
    return (y * g.astype(jnp.float32)).astype(x.dtype)

def project(xn, w_in, qn_a, kn_a, qn_b, kn_b, lb):
    B, T, _ = xn.shape
    p = jnp.einsum('btd,de->bte', xn, w_in)
    qa, ka, va, qb, kb, vb, qc, fc, ic, gc = jnp.split(p, SPLITS, axis=-1)
    qa = rmsnorm(qa.reshape(B, T, H_A, D_HEAD), qn_a)
    ka = rmsnorm(ka.reshape(B, T, H_A, D_HEAD), kn_a)
    va = va.reshape(B, T, H_A, D_HEAD)
    qb = rmsnorm(qb.reshape(B, T, H_B, D_HEAD), qn_b)
    kb = rmsnorm(kb.reshape(B, T, H_B, D_HEAD), kn_b)
    vb = vb.reshape(B, T, H_B, D_HEAD)
    f_raw = fc.astype(jnp.float32)
    log_f = jnp.logaddexp(jnp.log(jnp.maximum(lb, LB_FLOOR)), jnp.log1p(-lb) + jax.nn.log_sigmoid(f_raw))
    k_c = (1.0 - lb) * jax.nn.sigmoid(-f_raw)
    q_c = qc.astype(jnp.float32) * (DK_C ** -0.5)
    q_c = q_c.reshape(B, T, H_C, DK_C)
    k_c = k_c.reshape(B, T, H_C, DK_C)
    log_f = log_f.reshape(B, T, H_C, DK_C)
    v_c = ic.reshape(B, T, H_C, DV_C)
    return (qa, ka, va), (qb, kb, vb), (q_c, k_c, v_c, log_f), gc

def stick_breaking_block(q, k, v, q_pos, k_pos):
    z = jnp.einsum('bqhd,bkhd->bhqk', q, k).astype(jnp.float32) / math.sqrt(D_HEAD)
    mask = k_pos[None, :] < q_pos[:, None]
    log_1m = jnp.where(mask, -jax.nn.softplus(z), 0.0)
    later = lax.cumsum(log_1m, axis=3, reverse=True) - log_1m
    w = jnp.where(mask, jnp.exp(jax.nn.log_sigmoid(z) + later), 0.0)
    return jnp.einsum('bhqk,bkhd->bqhd', w.astype(v.dtype), v)

def sb_prompt(q, k, v):
    B, T = q.shape[:2]
    nb = T // Q_BLOCK
    pos = jnp.arange(T)
    qb = jnp.moveaxis(q.reshape(B, nb, Q_BLOCK, H_A, D_HEAD), 1, 0)
    pb = pos.reshape(nb, Q_BLOCK)
    out = lax.map(lambda a: stick_breaking_block(a[0], k, v, a[1], pos), (qb, pb))
    return jnp.moveaxis(out, 0, 1).reshape(B, T, H_A, D_HEAD)

def rel_bias(table, dist):
    idx = jnp.clip(dist, -REL_CLIP, REL_CLIP) + REL_CLIP
    return table.astype(jnp.float32)[:, idx]

def chunk_band_prompt(q, k, v, table):
    B, T = q.shape[:2]
    nc = T // CHUNK
    pad = ((0, 0), (N_PREV_CHUNKS, 0), (0, 0), (0, 0), (0, 0))
    qc = q.reshape(B, nc, CHUNK, H_B, D_HEAD)
    kp = jnp.pad(k.reshape(B, nc, CHUNK, H_B, D_HEAD), pad)
    vp = jnp.pad(v.reshape(B, nc, CHUNK, H_B, D_HEAD), pad)
    idx = jnp.arange(nc)[:, None] + jnp.arange(BAND)[None, :]
    kb = kp[:, idx].reshape(B, nc, BAND * CHUNK, H_B, D_HEAD)
    vb = vp[:, idx].reshape(B, nc, BAND * CHUNK, H_B, D_HEAD)
    s = jnp.einsum('bcqhd,bckhd->bchqk', qc, kb).astype(jnp.float32) / math.sqrt(D_HEAD)
    i = jnp.arange(CHUNK)
    m = jnp.arange(BAND * CHUNK)
    dist = N_PREV_CHUNKS * CHUNK + i[:, None] - m[None, :]
    valid = (jnp.arange(nc)[:, None] - N_PREV_CHUNKS + m[None, :] // CHUNK) >= 0
    s = s + rel_bias(table, dist)[None, None]
    s = jnp.where(valid[None, :, None, None, :], s, NEG_BIG)
    p = jax.nn.softmax(s, axis=-1)
    o = jnp.einsum('bchqk,bckhd->bcqhd', p.astype(v.dtype), vb)
    return o.reshape(B, T, H_B, D_HEAD)

def chunk_band_sample(q, k_new, v_new, cache_k, cache_v, table, past_len):
    Lb = cache_k.shape[1]
    T = q.shape[1]
    k = jnp.concatenate([cache_k, k_new], axis=1)
    v = jnp.concatenate([cache_v, v_new], axis=1)
    q_pos = past_len + jnp.arange(T)
    k_pos = jnp.concatenate([past_len - Lb + jnp.arange(Lb), q_pos])
    s = jnp.einsum('bqhd,bkhd->bhqk', q, k).astype(jnp.float32) / math.sqrt(D_HEAD)
    qch = q_pos // CHUNK
    kch = k_pos // CHUNK
    valid = (kch[None, :] >= qch[:, None] - N_PREV_CHUNKS) & (kch[None, :] <= qch[:, None])
    s = s + rel_bias(table, q_pos[:, None] - k_pos[None, :])[None]
    s = jnp.where(valid[None, None], s, NEG_BIG)
    p = jax.nn.softmax(s, axis=-1)
    return jnp.einsum('bhqk,bkhd->bqhd', p.astype(v.dtype), v)

def hgrn2_block(S, xs):
    q, k, v, log_f = xs
    L = q.shape[1]
    G = jnp.cumsum(log_f, axis=1)
    causal = jnp.tril(jnp.ones((L, L), dtype=bool))[None, :, :, None, None]
    diff = G[:, :, None] - G[:, None, :]
    decay = jnp.where(causal, jnp.exp(jnp.minimum(diff, 0.0)), 0.0)
    A = jnp.einsum('bihk,bjhk,bijhk->bhij', q, k, decay)
    o = jnp.einsum('bhij,bjhv->bihv', A, v) + jnp.einsum('bihk,bhkv->bihv', q * jnp.exp(G), S)
    G_last = G[:, -1]
    k_dec = k * jnp.exp(G_last[:, None] - G)
    S_new = jnp.exp(G_last)[..., None] * S + jnp.einsum('bjhk,bjhv->bhkv', k_dec, v)
    return S_new, o

def hgrn2_scan(S0, q, k, v, log_f, block):
    B, T = q.shape[:2]
    nb = T // block

    def blocks(a):
        return jnp.moveaxis(a.reshape(B, nb, block, *a.shape[2:]), 1, 0)

    S, o = lax.scan(hgrn2_block, S0.astype(jnp.float32),
                    (blocks(q), blocks(k), blocks(v.astype(jnp.float32)), blocks(log_f)))
    o = jnp.moveaxis(o, 0, 1).reshape(B, T, H_C, DV_C)
    return o.astype(v.dtype), S

def merge_and_ffn(x, oa, ob, oc, gc, onorm_c, w_o, norm_ffn, w_up, w_down):
    B, T, _ = x.shape
    oc = rmsnorm(oc, onorm_c).reshape(B, T, W_C) * jax.nn.silu(gc)
    mixed = jnp.concatenate([oa.reshape(B, T, W_A), ob.reshape(B, T, W_B), oc.astype(x.dtype)], axis=-1)
    h = x + jnp.einsum('bte,ed->btd', mixed, w_o)
    u = jax.nn.relu(jnp.einsum('btd,df->btf', rmsnorm(h, norm_ffn), w_up))
    return h + jnp.einsum('btf,fd->btd', u * u, w_down)

def setup_inputs(seed: int = 0) -> dict:
    key = jax.random.key(seed)
    ks = jax.random.split(key, 20)
    f32 = jnp.float32

    def nrm(k, shape, scale):
        return scale * jax.random.normal(k, shape, f32)

    band_rows = min(N_PREV_CHUNKS * CHUNK, PAST_LEN)
    return {
        "x_prompt": nrm(ks[0], (BATCH, SEQ, D_MODEL), 1.0),
        "x_sample": nrm(ks[1], (DEC_BATCH, DEC_SEQ, D_MODEL), 1.0),
        "cache_a_k": nrm(ks[2], (DEPTH, DEC_BATCH, PAST_LEN, H_A, D_HEAD), 1.0),
        "cache_a_v": nrm(ks[3], (DEPTH, DEC_BATCH, PAST_LEN, H_A, D_HEAD), 1.0),
        "cache_b_k": nrm(ks[4], (DEPTH, DEC_BATCH, band_rows, H_B, D_HEAD), 1.0),
        "cache_b_v": nrm(ks[5], (DEPTH, DEC_BATCH, band_rows, H_B, D_HEAD), 1.0),
        "state_c": nrm(ks[6], (DEPTH, DEC_BATCH, H_C, DK_C, DV_C), 0.5),
        "norm_mix": 1.0 + nrm(ks[7], (DEPTH, D_MODEL), 0.02),
        "w_in": nrm(ks[8], (DEPTH, D_MODEL, D_IN), D_MODEL ** -0.5),
        "qnorm_a": 1.0 + nrm(ks[9], (DEPTH, D_HEAD), 0.02),
        "knorm_a": 1.0 + nrm(ks[10], (DEPTH, D_HEAD), 0.02),
        "qnorm_b": 1.0 + nrm(ks[11], (DEPTH, D_HEAD), 0.02),
        "knorm_b": 1.0 + nrm(ks[12], (DEPTH, D_HEAD), 0.02),
        "rel_bias_b": nrm(ks[13], (DEPTH, H_B, N_REL), 0.1),
        "lower_bounds": nrm(ks[14], (DEPTH, QK_C), 0.1),
        "onorm_c": 1.0 + nrm(ks[15], (DEPTH, DV_C), 0.02),
        "w_o": nrm(ks[16], (DEPTH, D_MIX, D_MODEL), D_MIX ** -0.5),
        "norm_ffn": 1.0 + nrm(ks[17], (DEPTH, D_MODEL), 0.02),
        "w_up": nrm(ks[18], (DEPTH, D_MODEL, D_FF), D_MODEL ** -0.5),
        "w_down": nrm(ks[19], (DEPTH, D_FF, D_MODEL), D_FF ** -0.5),
    }

def reference(x_prompt, x_sample, cache_a_k, cache_a_v, cache_b_k, cache_b_v, state_c,
              norm_mix, w_in, qnorm_a, knorm_a, qnorm_b, knorm_b, rel_bias_b, lower_bounds,
              onorm_c, w_o, norm_ffn, w_up, w_down):
    lb_sm = jax.nn.softmax(lower_bounds.astype(jnp.float32), axis=0)
    lb_all = jnp.cumsum(lb_sm, axis=0) - lb_sm[0]
    past_len = cache_a_k.shape[2]
    Bp, Tp = x_prompt.shape[:2]
    Bs, Ts = x_sample.shape[:2]
    band_rows_p = min(N_PREV_CHUNKS * CHUNK, Tp)
    q_pos_s = past_len + jnp.arange(Ts)
    k_pos_s = jnp.arange(past_len + Ts)

    xp, xs = x_prompt, x_sample
    akp, avp, bkp, bvp, csp = [], [], [], [], []
    aks, avs, bks, bvs, css = [], [], [], [], []
    for l in range(DEPTH):
        (qa, ka, va), (qb, kb, vb), (qc, kc, vc, lf), gc = project(
            rmsnorm(xp, norm_mix[l]), w_in[l], qnorm_a[l], knorm_a[l], qnorm_b[l], knorm_b[l], lb_all[l])
        oa = sb_prompt(qa, ka, va)
        ob = chunk_band_prompt(qb, kb, vb, rel_bias_b[l])
        oc, Sp = hgrn2_scan(jnp.zeros((Bp, H_C, DK_C, DV_C), jnp.float32), qc, kc, vc, lf, CHUNK)
        xp = merge_and_ffn(xp, oa, ob, oc, gc, onorm_c[l], w_o[l], norm_ffn[l], w_up[l], w_down[l])
        akp.append(ka)
        avp.append(va)
        bkp.append(kb[:, Tp - band_rows_p:])
        bvp.append(vb[:, Tp - band_rows_p:])
        csp.append(Sp.astype(x_prompt.dtype))

        (qa, ka, va), (qb, kb, vb), (qc, kc, vc, lf), gc = project(
            rmsnorm(xs, norm_mix[l]), w_in[l], qnorm_a[l], knorm_a[l], qnorm_b[l], knorm_b[l], lb_all[l])
        oa = stick_breaking_block(qa, jnp.concatenate([cache_a_k[l], ka], axis=1),
                                  jnp.concatenate([cache_a_v[l], va], axis=1), q_pos_s, k_pos_s)
        ob = chunk_band_sample(qb, kb, vb, cache_b_k[l], cache_b_v[l], rel_bias_b[l], past_len)
        oc, Ss = hgrn2_scan(state_c[l], qc, kc, vc, lf, Ts)
        xs = merge_and_ffn(xs, oa, ob, oc, gc, onorm_c[l], w_o[l], norm_ffn[l], w_up[l], w_down[l])
        aks.append(ka)
        avs.append(va)
        bks.append(kb)
        bvs.append(vb)
        css.append(Ss.astype(x_sample.dtype))

    a_k_prompt = jnp.stack(akp)
    a_v_prompt = jnp.stack(avp)
    b_k_prompt = jnp.stack(bkp)
    b_v_prompt = jnp.stack(bvp)
    c_state_prompt = jnp.stack(csp)
    a_k_sample = jnp.stack(aks)
    a_v_sample = jnp.stack(avs)
    b_k_sample = jnp.stack(bks)
    b_v_sample = jnp.stack(bvs)
    c_state_sample = jnp.stack(css)
    return (xp, xs, a_k_prompt, a_v_prompt, b_k_prompt, b_v_prompt, c_state_prompt,
            a_k_sample, a_v_sample, b_k_sample, b_v_sample, c_state_sample)


_drawn_inputs = setup_inputs


def setup_inputs(seed=0):
    import zlib

    import numpy as np

    out = dict(_drawn_inputs(seed))
    spreads = {}
    factors = {'norm_mix': 2.728,
     'qnorm_a': 64.0,
     'qnorm_b': 30.86,
     'knorm_b': 9.622,
     'rel_bias_b': 8.0,
     'onorm_c': 6.894,
     'norm_ffn': 10.075,
     'cache_a_k': 5.618,
     'cache_a_v': 4.454,
     'cache_b_k': 8.0,
     'cache_b_v': 8.0}
    for name, (base, spread) in spreads.items():
        noise = np.random.default_rng([zlib.crc32(name.encode()), seed]).standard_normal(out[name].shape)
        drawn = base * np.exp(spread * noise) if base else spread * noise
        out[name] = __import__('jax').numpy.asarray(drawn.astype(out[name].dtype))
    for name, factor in factors.items():
        out[name] = (out[name] * factor).astype(out[name].dtype)
    return out
```

```python
from contextlib import ExitStack

import concourse.bass as bass
from concourse import mybir

F32 = mybir.dt.float32
F32R = mybir.dt.float32r
I32 = mybir.dt.int32
ALU = mybir.AluOpType
ACT = mybir.ActivationFunctionType
AX = mybir.AxisListType

P = 128
D = 1024
KD = D // P
SEQ, NEW, PAST = 2048, 32, 512
T = SEQ + NEW
NT = SEQ // P
DH, H = 64, 4
WH = H * DH
G = 512
NG = 7
DFF = 4 * D
CHUNK, PREV = 64, 8
CLIP = 128
BW = PREV * CHUNK + P
NLINE = BW + P - 1
EPS = 1e-6
NEG = -1e30
TILES = [(t * P, P) for t in range(NT)] + [(SEQ, NEW)]
HALVES = [TILES[:NT // 2], TILES[NT // 2:]]
THIRDS = [TILES[0:6], TILES[6:12], TILES[12:]]
QKA, VQ, KV, QC, FC, IC, GC = range(NG)


def blocks_of(n):
    k = -(-n // 512)
    while n % k:
        k += 1
    return [(i * (n // k), n // k) for i in range(k)]


class Space:

    def __init__(self, nc, ctx):
        self.nc, self.ctx = nc, ctx

    def sb(self, name, shape, dt=F32):
        return self.ctx.enter_context(self.nc.sbuf_tensor(name, shape, dt))

    def ps(self, name, shape):
        return self.ctx.enter_context(self.nc.psum_tensor(name, shape, F32))

    def sem(self, name):
        return self.ctx.enter_context(self.nc.semaphore(name))


def bcast_rows(ap, rows):
    return ap.rearrange("(a n) -> a n", a=1).to_broadcast([rows, ap.shape[0]])


def project(nc, x, norm_mix, w_in, gains, proj, tr, outs):
    ctx = ExitStack()
    with ctx:
        S = Space(nc, ctx)
        ident = S.sb("pj_ident", [P, P])
        grow = S.sb("pj_grow", [P, D])
        gain = S.sb("pj_gain", [P, 4, DH])
        minus_half = S.sb("pj_mhalf", [P, 8])
        xin = [S.sb(f"pj_xin{i}", [P, D]) for i in range(2)]
        xs = [S.sb(f"pj_xs{i}", [P, D]) for i in range(2)]
        ss = S.sb("pj_ss", [P, len(TILES)])
        rstd = S.sb("pj_rstd", [P, len(TILES)])
        HT = max(sum(r for _, r in h) for h in HALVES)
        xhi = S.sb("pj_xhi", [P, KD, HT], F32R)
        xlo = S.sb("pj_xlo", [P, KD, HT], F32R)
        wst = S.sb("pj_wst", [P, KD, G])
        whi = [S.sb(f"pj_whi{i}", [P, KD, G], F32R) for i in range(2)]
        wlo = [S.sb(f"pj_wlo{i}", [P, KD, G], F32R) for i in range(2)]
        NO = 4
        sq = [S.sb(f"pj_sq{i}", [P, G]) for i in range(NO)]
        ob = [S.sb(f"pj_ob{i}", [P, G]) for i in range(NO)]
        hs = [S.sb(f"pj_hs{i}", [P, 8]) for i in range(NO)]
        hr = [S.sb(f"pj_hr{i}", [P, 8]) for i in range(NO)]
        psT = [S.ps(f"pj_psT{i}", [P, KD, P]) for i in range(2)]
        psO = [S.ps(f"pj_psO{i}", [P, G]) for i in range(NO)]
        consts = S.sem("pj_consts")
        ident_step = S.sem("pj_ident_step")
        x_loaded = [S.sem(f"pj_x_loaded{i}") for i in range(2)]
        squared = S.sem("pj_squared")
        mean_ready = S.sem("pj_mean_ready")
        rstd_ready = S.sem("pj_rstd_ready")
        xs_ready = S.sem("pj_xs_ready")
        xT_ready = S.sem("pj_xT_ready")
        xhi_ready = S.sem("pj_xhi_ready")
        xlo_ready = S.sem("pj_xlo_ready")
        w_loaded = S.sem("pj_w_loaded")
        whi_ready = S.sem("pj_whi_ready")
        wlo_ready = S.sem("pj_wlo_ready")
        unit_done = S.sem("pj_unit_done")
        act_evac = S.sem("pj_act_evac")
        sums_ready = S.sem("pj_sums_ready")
        hmean_ready = S.sem("pj_hmean_ready")
        hrstd_ready = S.sem("pj_hrstd_ready")
        scaled = S.sem("pj_scaled")
        dve_evac = S.sem("pj_dve_evac")
        stored = [S.sem(f"pj_stored{i}") for i in range(NO)]

        units, first_tile = [], [0, len(HALVES[0])]
        for hf, tiles in enumerate(HALVES):
            base = tiles[0][0]
            n = sum(r for _, r in tiles)
            for g in range(NG):
                if g in (QC, FC):
                    for e in range(G // P):
                        for c0, cn in blocks_of(n):
                            units.append((hf, g, e, base + c0, cn))
                else:
                    for t0, r in tiles:
                        units.append((hf, g, 0, t0, r))
        NORMED = {QKA: (0, 8, 0), VQ: (WH, 4, 2), KV: (0, 4, 3)}
        BY_DVE = (QKA, VQ, KV, GC)

        def units_upto_group(m):
            return sum(1 for u in units if u[0] * NG + u[1] <= m)

        def dve_units(n):
            return sum(1 for u in units[:n + 1] if u[1] in BY_DVE)

        def normed_units(n):
            return sum(1 for u in units[:n + 1] if u[1] in NORMED)

        def wait_whole(eng, n):
            if units[n][1] in BY_DVE:
                eng.wait_ge(dve_evac, dve_units(n))
            else:
                eng.wait_ge(act_evac, n + 1)

        def stores(n):
            hf, g, e, t0, r = units[n]
            if g == QC:
                return [(tr[0, e, :, t0:t0 + r], (slice(0, P), slice(0, r)), 0)]
            if g == FC:
                return [(tr[1, e, :, t0:t0 + r], (slice(0, P), slice(0, r)), 0),
                        (tr[2, e, :, t0:t0 + r], (slice(0, P), slice(0, r)), 1)]
            out = [(proj[g, t0:t0 + r, :], (slice(0, r), slice(0, G)), 0)]
            for name, gg, c in (("ak", QKA, WH), ("av", VQ, 0), ("bk", KV, 0), ("bv", KV, WH)):
                if g != gg:
                    continue
                if t0 == SEQ:
                    dst = outs[name + "s"]
                elif name[0] == "a":
                    dst = outs[name + "p"][t0:t0 + r, :]
                elif t0 >= SEQ - PREV * CHUNK:
                    q = t0 - (SEQ - PREV * CHUNK)
                    dst = outs[name + "p"][q:q + r, :]
                else:
                    continue
                out.append((dst, (slice(0, r), slice(c, c + WH)), 0))
            return out

        def stored_count(n):
            return 16 * sum(len(stores(k)) for k in range(n % NO, n + 1, NO))

        block = ctx.enter_context(nc.Block())

        def load_w(sp, hf, g):
            m = hf * NG + g
            if m >= 1:
                sp.wait_ge(whi_ready, m)
                sp.wait_ge(wlo_ready, m)
            sp.dma_start(wst[:, :, :], w_in[:, g * G:(g + 1) * G].rearrange("(k p) n -> p k n", p=P)
                         ).then_inc(w_loaded, 16)

        @block.sync
        def _(sp):
            sp.dma_start(grow[:, :], bcast_rows(norm_mix, P)).then_inc(consts, 16)
            for i, g in enumerate(gains):
                sp.dma_start(gain[:, i, :], bcast_rows(g, P)).then_inc(consts, 16)
            for hf, tiles in enumerate(HALVES):
                for i, (t0, r) in enumerate(tiles):
                    n = first_tile[hf] + i
                    if n >= 2:
                        sp.wait_ge(xs_ready, n - 1)
                    sp.dma_start(xin[n % 2][0:r, :], x(t0, r)).then_inc(x_loaded[n % 2], 16)
                    if i == 1:
                        load_w(sp, hf, 0)
                load_w(sp, hf, 1)
                for n, (uh, g, e, t0, r) in enumerate(units):
                    if uh != hf:
                        continue
                    wait_whole(sp, n)
                    for dst, (ps_, cs), which in stores(n):
                        src = (ob, sq)[which][n % NO]
                        sp.dma_start(dst, src[ps_, cs]).then_inc(stored[n % NO], 16)
                    if g + 2 < NG and (n == 0 or units[n - 1][:2] != (uh, g)):
                        load_w(sp, hf, g + 2)
            for n in range(len(units) - NO, len(units)):
                sp.wait_ge(stored[n % NO], stored_count(n))

        @block.gpsimd
        def _(pool):
            nc.gpsimd.memset(ident[:, :], 0.0).then_inc(ident_step, 1)
            nc.gpsimd.memset(minus_half[:, :], -0.5).then_inc(ident_step, 1)
            pool.wait_ge(ident_step, 2)
            nc.gpsimd.affine_select(out=ident[:, :], in_=ident[:, :], compare_op=ALU.not_equal, fill=1.0,
                                    base=0, pattern=[[-1, P]], channel_multiplier=1).then_inc(ident_step, 1)
            for hf, tiles in enumerate(HALVES):
                for i, (t0, r) in enumerate(tiles):
                    n = first_tile[hf] + i
                    pool.wait_ge(squared, n + 1)
                    nc.gpsimd.tensor_scalar(rstd[0:r, n:n + 1], ss[0:r, n:n + 1], 1.0 / D, EPS,
                                            ALU.mult, ALU.add).then_inc(mean_ready, 1)
                    pool.wait_ge(mean_ready, n + 1)
                    nc.gpsimd.tensor_tensor(rstd[0:r, n:n + 1], rstd[0:r, n:n + 1], minus_half[0:r, 0:1],
                                            ALU.pow).then_inc(rstd_ready, 1)
                for n, (uh, g, e, t0, r) in enumerate(units):
                    if uh == hf:
                        if g in NORMED:
                            k = normed_units(n)
                            c, nh, _ = NORMED[g]
                            b = n % NO
                            pool.wait_ge(sums_ready, k)
                            nc.gpsimd.tensor_scalar(hr[b][0:r, 0:nh], hs[b][0:r, 0:nh], 1.0 / DH, EPS,
                                                    ALU.mult, ALU.add).then_inc(hmean_ready, 1)
                            pool.wait_ge(hmean_ready, k)
                            nc.gpsimd.tensor_tensor(hr[b][0:r, 0:nh], hr[b][0:r, 0:nh],
                                                    minus_half[0:r, 0:nh], ALU.pow).then_inc(hrstd_ready, 1)

        @block.scalar
        def _(act):
            def split_w(m):
                act.wait_ge(w_loaded, 16 * (m + 1))
                if m >= 2:
                    act.wait_ge(unit_done, units_upto_group(m - 2))
                nc.scalar.activation(whi[m % 2][:, :, :], wst[:, :, :], ACT.Copy).then_inc(whi_ready, 1)

            for hf, tiles in enumerate(HALVES):
                base = tiles[0][0]
                for i, (t0, r) in enumerate(tiles):
                    n = first_tile[hf] + i
                    act.wait_ge(x_loaded[n % 2], 16 * (n // 2 + 1))
                    if n >= 2:
                        act.wait_ge(xT_ready, n - 1)
                    nc.scalar.activation(xs[n % 2][0:r, :], xin[n % 2][0:r, :], ACT.Square,
                                         accum_out=ss[0:r, n:n + 1]).then_inc(squared, 1)
                    if hf == 1 and i == 0:
                        act.wait_ge(unit_done, units_upto_group(NG - 1))
                    act.wait_ge(xT_ready, n + 1)
                    nc.scalar.activation(xhi[:, :, t0 - base:t0 - base + r], psT[n % 2][:, :, 0:r],
                                         ACT.Copy).then_inc(xhi_ready, 1)
                    if i == 1:
                        split_w(hf * NG)
                for n, (uh, g, e, t0, r) in enumerate(units):
                    if uh != hf:
                        continue
                    if n == 0 or units[n - 1][:2] != (uh, g):
                        if g + 1 < NG:
                            split_w(hf * NG + g + 1)
                    b = n % NO
                    rows, cols = (P, r) if g in (QC, FC) else (r, G)
                    act.wait_ge(unit_done, n + 1)
                    if n >= NO:
                        act.wait_ge(stored[b], stored_count(n - NO))
                    if g in NORMED:
                        last = nc.scalar.activation(sq[b][0:r, :], psO[b][0:r, :], ACT.Square)
                    elif g == GC:
                        last = nc.scalar.activation(sq[b][0:r, :], psO[b][0:r, :], ACT.Sigmoid)
                    elif g == FC:
                        nc.scalar.activation(ob[b][:, 0:r], psO[b][:, 0:r], ACT.Sigmoid)
                        last = nc.scalar.activation(sq[b][:, 0:r], psO[b][:, 0:r], ACT.Sigmoid, scale=-1.0)
                    elif g == QC:
                        last = nc.scalar.activation(ob[b][:, 0:r], psO[b][:, 0:r], ACT.Copy,
                                                    scale=float(P) ** -0.5)
                    else:
                        last = nc.scalar.activation(ob[b][0:r, :], psO[b][0:r, :], ACT.Copy)
                    last.then_inc(act_evac, 1)

        @block.vector
        def _(dve):
            def split_w(m):
                dve.wait_ge(whi_ready, m + 1)
                if m >= 2:
                    dve.wait_ge(unit_done, units_upto_group(m - 2))
                nc.vector.tensor_tensor(wlo[m % 2][:, :, :], wst[:, :, :], whi[m % 2][:, :, :].bitcast(F32),
                                        ALU.subtract).then_inc(wlo_ready, 1)

            dve.wait_ge(consts, 16 * 5)
            for hf, tiles in enumerate(HALVES):
                base = tiles[0][0]
                for i, (t0, r) in enumerate(tiles):
                    n = first_tile[hf] + i
                    dve.wait_ge(rstd_ready, n + 1)
                    nc.vector.scalar_tensor_tensor(out=xs[n % 2][0:r, :], in0=xin[n % 2][0:r, :],
                                                   scalar=rstd[0:r, n:n + 1], in1=grow[0:r, :],
                                                   op0=ALU.mult, op1=ALU.mult).then_inc(xs_ready, 1)
                    dve.wait_ge(xhi_ready, n + 1)
                    cs = slice(t0 - base, t0 - base + r)
                    nc.vector.tensor_tensor(xlo[:, :, cs], psT[n % 2][:, :, 0:r],
                                            xhi[:, :, cs].bitcast(F32), ALU.subtract).then_inc(xlo_ready, 1)
                    if i == 1:
                        split_w(hf * NG)
                for n, (uh, g, e, t0, r) in enumerate(units):
                    if uh != hf:
                        continue
                    if n == 0 or units[n - 1][:2] != (uh, g):
                        if g + 1 < NG:
                            split_w(hf * NG + g + 1)
                    b = n % NO
                    if g not in BY_DVE:
                        continue
                    dve.wait_ge(act_evac, n + 1)
                    if g in NORMED:
                        k = normed_units(n)
                        c, nh, gi = NORMED[g]
                        seg = slice(c, c + nh * DH)
                        nc.vector.tensor_reduce(hs[b][0:r, 0:nh],
                                                sq[b][0:r, seg].rearrange("p (h d) -> p h d", d=DH),
                                                axis=AX.X, op=ALU.add).then_inc(sums_ready, 1)
                        if nh == 4:
                            other = slice(WH - c, 2 * WH - c)
                            nc.vector.tensor_copy(ob[b][0:r, other], psO[b][0:r, other])
                        dve.wait_ge(hrstd_ready, k)
                        o3 = ob[b][0:r, seg].rearrange("p (h d) -> p h d", d=DH)
                        nc.vector.tensor_tensor(o3, psO[b][0:r, seg].rearrange("p (h d) -> p h d", d=DH),
                                                hr[b][0:r, 0:nh].unsqueeze(2).to_broadcast([r, nh, DH]),
                                                ALU.mult).then_inc(scaled, 1)
                        dve.wait_ge(scaled, k)
                        if nh == 8:
                            o4 = ob[b][0:r, :].rearrange("p (a h d) -> p a h d", a=2, d=DH)
                            last = nc.vector.tensor_tensor(
                                o4, o4, gain[0:r, 0:2, :].unsqueeze(2).to_broadcast([r, 2, 4, DH]), ALU.mult)
                        else:
                            last = nc.vector.tensor_tensor(
                                o3, o3, gain[0:r, gi:gi + 1, :].to_broadcast([r, nh, DH]), ALU.mult)
                    else:
                        last = nc.vector.tensor_tensor(ob[b][0:r, :], psO[b][0:r, :], sq[b][0:r, :], ALU.mult)
                    last.then_inc(dve_evac, 1)

        @block.tensor
        def _(pe):
            pe.wait_ge(ident_step, 3)
            for hf, tiles in enumerate(HALVES):
                base = tiles[0][0]
                for i, (t0, r) in enumerate(tiles):
                    n = first_tile[hf] + i
                    pe.wait_ge(xs_ready, n + 1)
                    if n >= 2:
                        pe.wait_ge(xlo_ready, n - 1)
                    for k in range(KD):
                        last = nc.tensor.transpose(psT[n % 2][:, k, 0:r], xs[n % 2][0:r, k * P:(k + 1) * P],
                                                   ident[0:r, 0:r])
                    last.then_inc(xT_ready, 1)
                pe.wait_ge(xlo_ready, first_tile[hf] + len(tiles))
                for n, (uh, g, e, t0, r) in enumerate(units):
                    if uh != hf:
                        continue
                    m = hf * NG + g
                    pe.wait_ge(wlo_ready, m + 1)
                    if n >= NO:
                        wait_whole(pe, n - NO)
                    c = slice(t0 - base, t0 - base + r)
                    passes = [(xhi, whi), (xhi, wlo), (xlo, whi)]
                    for k in range(KD):
                        for j, (xa, wa) in enumerate(passes):
                            st, sp_ = k == 0 and j == 0, k == KD - 1 and j == 2
                            wt = wa[m % 2]
                            if g in (QC, FC):
                                last = nc.tensor.matmul(psO[n % NO][:, 0:r], wt[:, k, e * P:(e + 1) * P],
                                                        xa[:, k, c], start=st, stop=sp_)
                            else:
                                last = nc.tensor.matmul(psO[n % NO][0:r, :], xa[:, k, c], wt[:, k, :],
                                                        start=st, stop=sp_)
                    last.then_inc(unit_done, 1)


def attend(nc, kind, q_src, k_src, v_src, bias, mix):
    A = kind == "A"
    SMP = PAST + NEW
    NC = PAST // P
    steps = [("s", j * P, P, False) for j in range(NC)] + [("s", PAST, NEW, True)]
    steps += [("p", j * P, P, True) for j in range(NT)]
    NSTEP = len(steps)
    kt0 = {"s": 0, "p": SMP}
    vt0 = {"s": 0, "p": NC + 1}
    units = []
    for s, (seq, t0, r, att) in enumerate(steps):
        if not att:
            continue
        for h in range(H):
            end = t0 + r
            if A:
                c = (end - 1) // 512
                while c >= 0:
                    c1 = min(end, 512 * (c + 1))
                    units.append((s, h, 512 * c, c1 - 512 * c, c1 == end, c == 0))
                    c -= 1
            else:
                k0 = max(0, t0 - PREV * CHUNK)
                units.append((s, h, k0, end - k0, True, True))
    NU = len(units)
    rows_of = [units[n][:2] for n in range(NU)]
    row_ids = sorted(set(rows_of))
    row_no = {x: i for i, x in enumerate(row_ids)}
    row_last = {row_no[rows_of[n]]: n for n in range(NU)}
    att_steps = [s for s in range(NSTEP) if steps[s][3]]
    att_no = {s: i for i, s in enumerate(att_steps)}
    step_last = {s: max(n for n in range(NU) if units[n][0] == s) for s in att_steps}
    step_first = {s: min(n for n in range(NU) if units[n][0] == s) for s in att_steps}
    TLAG = 3 if A else 2
    ctx = ExitStack()
    with ctx:
        S = Space(nc, ctx)
        pre = "at" + kind
        ZB = 4 if A else 2
        ZW = 512 if A else 1024
        WB = 2 if A else 1
        WW = 4 if A else 5
        NW = 3
        ident = S.sb(pre + "ident", [P, P])
        kn = [S.sb(pre + f"kn{i}", [P, H, DH]) for i in range(2)]
        qn = [S.sb(pre + f"qn{i}", [P, H, 2, DH]) for i in range(2)]
        khl = [S.sb(pre + f"khl{i}", [P, H, 2, DH]) for i in range(2)]
        KT = S.sb(pre + "KT", [P, H, SMP + SEQ], F32R)
        V = S.sb(pre + "V", [P, NC + 1 + NT, WH])
        qhi = [S.sb(pre + f"qhi{i}", [P, H, P], F32R) for i in range(2)]
        qlo = [S.sb(pre + f"qlo{i}", [P, H, P], F32R) for i in range(2)]
        ub = [S.sb(pre + f"ub{i}", [P, 512 if A else BW]) for i in range(NW)]
        wb = [S.sb(pre + f"wb{i}", [P, 512 if A else BW]) for i in range(NW)]
        wT = [S.sb(pre + f"wT{i}", [P, WW, P]) for i in range(2)]
        o = [S.sb(pre + f"o{i}", [P, WH]) for i in range(2)]
        if A:
            cp = [S.sb(pre + f"cp{i}", [P, SEQ + 1]) for i in range(2)]
        else:
            bt = S.sb(pre + "bt", [P, H, BW])
            btr = S.sb(pre + "btr", [P, H, BW])
            turn = S.sb(pre + "turn", [P, P])
            tb = S.sb(pre + "tb", [H, 2 * CLIP + 1])
            ln = S.sb(pre + "ln", [H, NLINE])
            mx = [S.sb(pre + f"mx{i}", [P, 1]) for i in range(NW)]
            nmx = [S.sb(pre + f"nmx{i}", [P, 1]) for i in range(NW)]
            den = [S.sb(pre + f"den{i}", [P, H]) for i in range(2)]
            rden = S.sb(pre + "rden", [P, H])
        psZ = [S.ps(pre + f"psZ{i}", [P, ZW]) for i in range(ZB)]
        psT = S.ps(pre + "psT", [P, H, P])
        psW = [S.ps(pre + f"psW{i}", [P, 4 if A else 8, P]) for i in range(WB)]
        psO = S.ps(pre + "psO", [P, WH])

        init = S.sem(pre + "init")
        loaded = [S.sem(pre + f"loaded{i}") for i in range(2)]
        bias_loaded = S.sem(pre + "bias_loaded")
        table_loaded = S.sem(pre + "table_loaded")
        line_ready = S.sem(pre + "line_ready")
        turned = S.sem(pre + "turned")
        bt_ready = S.sem(pre + "bt_ready")
        line_stored = S.sem(pre + "line_stored")
        khi_ready = S.sem(pre + "khi_ready")
        khl_ready = S.sem(pre + "khl_ready")
        kT_ready = S.sem(pre + "kT_ready")
        kT_out = S.sem(pre + "kT_out")
        qT_ready = S.sem(pre + "qT_ready")
        qhi_ready = S.sem(pre + "qhi_ready")
        qlo_ready = S.sem(pre + "qlo_ready")
        z_ready = S.sem(pre + "z_ready")
        u_ready = S.sem(pre + "u_ready")
        masked = S.sem(pre + "masked")
        scanned = S.sem(pre + "scanned")
        w_ready = S.sem(pre + "w_ready")
        wT_ready = S.sem(pre + "wT_ready")
        wT_out = S.sem(pre + "wT_out")
        av_done = S.sem(pre + "av_done")
        o_ready = S.sem(pre + "o_ready")
        max_ready = S.sem(pre + "max_ready")
        bias_added = S.sem(pre + "bias_added")
        nmax_ready = S.sem(pre + "nmax_ready")
        rden_ready = S.sem(pre + "rden_ready")
        stored = [S.sem(pre + f"stored{i}") for i in range(2)]

        def loads_upto(s):
            return 16 * sum(4 if steps[k][3] else 2 for k in range(s % 2, s + 1, 2))

        def att_upto(s):
            return sum(1 for k in att_steps if k <= s)

        def masks_upto(n):
            return sum(1 for u in units[:n + 1] if u[4])

        def slots():
            for s in range(NSTEP):
                if s == 0:
                    yield "prep", 0
                if s + 1 < NSTEP:
                    yield "prep", s + 1
                if steps[s][3]:
                    for n in range(step_first[s], step_last[s] + 1):
                        yield "unit", n
            for n in range(NU, NU + 6):
                yield "unit", n

        block = ctx.enter_context(nc.Block())

        @block.sync
        def _(sp):
            if not A:
                table, line = bias
                sp.dma_start(tb[:, :], table).then_inc(table_loaded, 16)
                sp.wait_ge(line_ready, 1)
                sp.dma_start(line, ln[:, :]).then_inc(line_stored, 16)
                sp.wait_ge(line_stored, 16)
                for h in range(H):
                    rows = bass.AP(line.tensor, line.offset + h * NLINE, [[1, P], [1, BW]])
                    sp.dma_start(btr[:, h, :], rows).then_inc(bias_loaded, 16)
            done = 0
            for what, i in slots():
                if what == "prep":
                    seq, t0, r, att = steps[i]
                    if i >= 2:
                        sp.wait_ge(khl_ready, i - 1)
                        if att_upto(i - 2):
                            sp.wait_ge(qT_ready, att_upto(i - 2))
                    sp.dma_start(kn[i % 2][0:r, :, :], k_src(seq, t0, r)).then_inc(loaded[i % 2], 16)
                    sp.dma_start(V[0:r, vt0[seq] + t0 // P, :], v_src(seq, t0, r)).then_inc(loaded[i % 2], 16)
                    if att:
                        for copy in range(2):
                            sp.dma_start(qn[i % 2][0:r, :, copy, :], q_src(seq, t0, r)).then_inc(loaded[i % 2], 16)
                elif done < len(att_steps) and i >= step_last[att_steps[done]] + 6 or i == NU + 5:
                    while done < len(att_steps) and (i >= step_last[att_steps[done]] + 6 or i == NU + 5):
                        seq, t0, r, _ = steps[att_steps[done]]
                        sp.wait_ge(o_ready, done + 1)
                        row = t0 if seq == "p" else SEQ
                        sp.dma_start(mix[row:row + r, :], o[done % 2][0:r, :]).then_inc(stored[done % 2], 16)
                        done += 1
            for i in range(2):
                sp.wait_ge(stored[i], 16 * len(range(i, len(att_steps), 2)))

        @block.gpsimd
        def _(pool):
            nc.gpsimd.memset(ident[:, :], 0.0).then_inc(init, 1)
            if A:
                for i in range(2):
                    nc.gpsimd.memset(cp[i][:, SEQ:SEQ + 1], 1.0).then_inc(init, 1)
                pool.wait_ge(init, 3)
            else:
                pool.wait_ge(init, 1)
            nc.gpsimd.affine_select(out=ident[:, :], in_=ident[:, :], compare_op=ALU.not_equal, fill=1.0,
                                    base=0, pattern=[[-1, P]], channel_multiplier=1).then_inc(init, 1)
            if not A:
                nc.gpsimd.memset(turn[:, :], 0.0).then_inc(init, 1)
                pool.wait_ge(init, 3)
                nc.gpsimd.affine_select(out=turn[:, :], in_=turn[:, :], compare_op=ALU.not_equal, fill=1.0,
                                        base=1 - P, pattern=[[1, P]], channel_multiplier=1).then_inc(init, 1)
                pool.wait_ge(init, 4)
                pool.wait_ge(bt_ready, H)
                nc.gpsimd.memset(bt[0:CHUNK, :, BW - CHUNK:BW], NEG).then_inc(init, 1)
                pool.wait_ge(init, 5)
                nc.gpsimd.memset(bt[CHUNK:P, :, 0:CHUNK], NEG).then_inc(init, 1)
                return
            for what, i in slots():
                if what != "unit":
                    continue
                if i < NU and units[i][4]:
                    s, h, k0, kn_, _, _ = units[i]
                    r = steps[s][2]
                    d = ub[i % NW][0:r, kn_ - r:kn_]
                    pool.wait_ge(u_ready, i + 1)
                    nc.gpsimd.affine_select(out=d, in_=d, compare_op=ALU.is_gt, fill=1.0, base=0,
                                            pattern=[[-1, r]], channel_multiplier=1).then_inc(masked, 1)

        @block.scalar
        def _(act):
            for what, i in slots():
                if what == "prep":
                    seq, t0, r, att = steps[i]
                    c = kt0[seq] + t0
                    act.wait_ge(kT_ready, i + 1)
                    nc.scalar.activation(KT[:, :, c:c + r], psT[:, :, 0:r], ACT.Copy).then_inc(kT_out, 1)
                    if att:
                        act.wait_ge(qT_ready, att_upto(i))
                        if att_no[i] >= 2:
                            act.wait_ge(z_ready, step_last[att_steps[att_no[i] - 2]] + 1)
                        b = att_no[i] % 2
                        nc.scalar.activation(qhi[b][:, :, 0:r], psT[:, :, 0:r], ACT.Copy).then_inc(qhi_ready, 1)
                    continue
                if i < NU:
                    s, h, k0, w, _, _ = units[i]
                    r = steps[s][2]
                    if A:
                        act.wait_ge(z_ready, i + 1)
                        if i >= NW:
                            act.wait_ge(scanned, i - NW + 1)
                        nc.scalar.activation(ub[i % NW][0:r, 0:w], psZ[i % ZB][0:r, 0:w], ACT.Sigmoid,
                                             scale=-float(DH) ** -0.5).then_inc(u_ready, 1)
                    else:
                        act.wait_ge(nmax_ready, i + 1)
                        if i >= NW:
                            act.wait_ge(wT_ready, i - NW + 1)
                        d = den[att_no[s] % 2]
                        if h == 0 and att_no[s] >= 2:
                            act.wait_ge(rden_ready, att_no[s] - 1)
                        nc.scalar.activation(wb[i % NW][0:r, 0:w], ub[i % NW][0:r, 0:w], ACT.Exp,
                                             bias=nmx[i % NW][0:r, :], accum_out=d[0:r, h:h + 1]
                                             ).then_inc(w_ready, 1)
                j = i - TLAG
                if 0 <= j < NU:
                    s, h, k0, w, _, _ = units[j]
                    r = steps[s][2]
                    act.wait_ge(wT_ready, j + 1)
                    if j >= 2:
                        act.wait_ge(av_done, j - 1)
                    full = w // P
                    last = None
                    if full:
                        last = nc.scalar.activation(wT[j % 2][:, 0:full, 0:r], psW[j % WB][:, 0:full, 0:r], ACT.Copy)
                    if w % P:
                        last = nc.scalar.activation(wT[j % 2][0:w % P, full, 0:r],
                                                    psW[j % WB][0:w % P, full, 0:r], ACT.Copy)
                    last.then_inc(wT_out, 1)

        @block.vector
        def _(dve):
            if not A:
                dve.wait_ge(table_loaded, 16)
                far = NLINE - 2 * CLIP
                nc.vector.tensor_copy(ln[:, 0:far], tb[:, 2 * CLIP:2 * CLIP + 1].to_broadcast([H, far]))
                nc.vector.tensor_copy(ln[:, far:NLINE], tb[:, 1:2 * CLIP + 1][:, ::-1]).then_inc(line_ready, 1)
                for h in range(H):
                    dve.wait_ge(turned, h + 1)
                    nc.vector.tensor_copy(bt[:, h, :], psZ[h % 2][:, 0:BW]).then_inc(bt_ready, 1)
            out_no = 0
            for what, i in slots():
                if what == "prep":
                    seq, t0, r, att = steps[i]
                    b = i % 2
                    dve.wait_ge(loaded[b], loads_upto(i))
                    if i >= 2:
                        dve.wait_ge(kT_ready, i - 1)
                    nc.vector.tensor_copy(khl[b][0:r, :, 0, :].bitcast(F32R), kn[b][0:r, :, :]).then_inc(khi_ready, 1)
                    dve.wait_ge(khi_ready, i + 1)
                    nc.vector.tensor_tensor(khl[b][0:r, :, 1, :], kn[b][0:r, :, :], khl[b][0:r, :, 0, :],
                                            ALU.subtract).then_inc(khl_ready, 1)
                    if att:
                        dve.wait_ge(qhi_ready, att_upto(i))
                        q = att_no[i] % 2
                        nc.vector.tensor_tensor(qlo[q][:, :, 0:r], psT[:, :, 0:r],
                                                qhi[q][:, :, 0:r].bitcast(F32), ALU.subtract).then_inc(qlo_ready, 1)
                    continue
                if i < NU:
                    s, h, k0, w, last_chunk, _ = units[i]
                    r, end = steps[s][2], steps[s][1] + steps[s][2]
                    u = ub[i % NW]
                    if A:
                        a = SEQ - end + k0
                        row = row_no[(s, h)]
                        c = cp[row % 2]
                        dve.wait_ge(u_ready, i + 1)
                        if last_chunk:
                            dve.wait_ge(masked, masks_upto(i))
                            if row >= 2:
                                dve.wait_ge(w_ready, row_last[row - 2] + 1)
                            init_v = 1.0
                        else:
                            dve.wait_ge(scanned, i)
                            init_v = c[0:r, a + w:a + w + 1]
                        nc.vector.tensor_tensor_scan(out=c[0:r, a:a + w][:, ::-1], data0=u[0:r, 0:w][:, ::-1],
                                                     data1=u[0:r, 0:w][:, ::-1], initial=init_v,
                                                     op0=ALU.mult, op1=ALU.bypass).then_inc(scanned, 1)
                    else:
                        dve.wait_ge(z_ready, i + 1)
                        if i == 0:
                            dve.wait_ge(init, 6)
                        if i >= NW:
                            dve.wait_ge(w_ready, i - NW + 1)
                        b0 = BW - w if steps[s][0] == "p" else 0
                        nc.vector.scalar_tensor_tensor(out=u[0:r, 0:w], in0=psZ[i % ZB][0:r, 0:w],
                                                       scalar=float(DH) ** -0.5, in1=bt[0:r, h, b0:b0 + w],
                                                       op0=ALU.mult, op1=ALU.add).then_inc(bias_added, 1)
                        dve.wait_ge(bias_added, i + 1)
                        nc.vector.tensor_reduce(mx[i % NW][0:r, :], u[0:r, 0:w], axis=AX.X,
                                                op=ALU.max).then_inc(max_ready, 1)
                        dve.wait_ge(max_ready, i + 1)
                        nc.vector.tensor_scalar(nmx[i % NW][0:r, :], mx[i % NW][0:r, :], -1.0, None,
                                                ALU.mult).then_inc(nmax_ready, 1)
                if A and 0 <= i - 1 < NU:
                    j = i - 1
                    s, h, k0, w, _, _ = units[j]
                    r, end = steps[s][2], steps[s][1] + steps[s][2]
                    a = SEQ - end + k0
                    c = cp[row_no[(s, h)] % 2]
                    dve.wait_ge(scanned, j + 1)
                    if j >= NW:
                        dve.wait_ge(wT_ready, j - NW + 1)
                    nc.vector.tensor_tensor(wb[j % NW][0:r, 0:w], c[0:r, a + 1:a + 1 + w],
                                            c[0:r, a:a + w], ALU.subtract).then_inc(w_ready, 1)
                if out_no < len(att_steps) and i >= step_last[att_steps[out_no]] + TLAG + 2:
                    s = att_steps[out_no]
                    r = steps[s][2]
                    dve.wait_ge(av_done, step_last[s] + 1)
                    if out_no >= 2:
                        dve.wait_ge(stored[out_no % 2], 16 * (out_no // 2))
                    ob = o[out_no % 2]
                    if A:
                        nc.vector.tensor_copy(ob[0:r, :], psO[0:r, :]).then_inc(o_ready, 1)
                    else:
                        nc.vector.reciprocal(rden[0:r, :], den[out_no % 2][0:r, :]).then_inc(rden_ready, 1)
                        dve.wait_ge(rden_ready, out_no + 1)
                        nc.vector.tensor_tensor(ob[0:r, :].rearrange("p (h d) -> p h d", h=H),
                                                psO[0:r, :].rearrange("p (h d) -> p h d", h=H),
                                                rden[0:r, :].unsqueeze(2).to_broadcast([r, H, DH]),
                                                ALU.mult).then_inc(o_ready, 1)
                    out_no += 1

        @block.tensor
        def _(pe):
            pe.wait_ge(init, 4)
            if not A:
                pe.wait_ge(bias_loaded, 16 * H)
                for h in range(H):
                    if h >= 2:
                        pe.wait_ge(bt_ready, h - 1)
                    for x0 in range(0, BW, 512):
                        x1 = min(BW, x0 + 512)
                        last = nc.tensor.matmul(psZ[h % 2][:, x0:x1], turn[:, :], btr[:, h, x0:x1],
                                                start=True, stop=True)
                    last.then_inc(turned, 1)
            for what, i in slots():
                if what == "prep":
                    seq, t0, r, att = steps[i]
                    b = i % 2
                    pe.wait_ge(khl_ready, i + 1)
                    if att_upto(i - 1):
                        pe.wait_ge(qlo_ready, att_upto(i - 1))
                    if i >= 1:
                        pe.wait_ge(kT_out, i)
                    for h in range(H):
                        last = nc.tensor.transpose(psT[:, h, 0:r], khl[b][0:r, h, :, :], ident[0:r, 0:r])
                    last.then_inc(kT_ready, 1)
                    if att:
                        pe.wait_ge(kT_out, i + 1)
                        for h in range(H):
                            last = nc.tensor.transpose(psT[:, h, 0:r], qn[b][0:r, h, :, :], ident[0:r, 0:r])
                        last.then_inc(qT_ready, 1)
                    continue
                if i < NU:
                    s, h, k0, w, _, _ = units[i]
                    seq, t0, r, _ = steps[s]
                    q = att_no[s] % 2
                    if i == step_first[s]:
                        pe.wait_ge(qlo_ready, att_upto(s))
                    if i == 0 and not A:
                        pe.wait_ge(bt_ready, H)
                    if i >= ZB:
                        if A:
                            pe.wait_ge(u_ready, i - ZB + 1)
                        else:
                            pe.wait_ge(bias_added, i - ZB + 1)
                    c0 = kt0[seq] + k0
                    for x0 in range(0, w, 512):
                        x1 = min(w, x0 + 512)
                        for qq, first in ((qhi, True), (qlo, False)):
                            last = nc.tensor.matmul(psZ[i % ZB][0:r, x0:x1], qq[q][:, h, 0:r],
                                                    KT[:, h, c0 + x0:c0 + x1], start=first, stop=not first)
                    last.then_inc(z_ready, 1)
                j = i - TLAG - 1
                if 0 <= j < NU:
                    s, h, k0, w, first, last_ = units[j]
                    seq, t0, r, _ = steps[s]
                    pe.wait_ge(wT_out, j + 1)
                    if j == step_first[s] and att_no[s] >= 1:
                        pe.wait_ge(o_ready, att_no[s])
                    nb = -(-w // P)
                    for b in range(nb):
                        kr = min(P, w - b * P)
                        last = nc.tensor.matmul(psO[0:r, h * DH:(h + 1) * DH], wT[j % 2][0:kr, b, 0:r],
                                                V[0:kr, vt0[seq] + k0 // P + b, h * DH:(h + 1) * DH],
                                                start=first and b == 0, stop=last_ and b == nb - 1)
                    last.then_inc(av_done, 1)
                j = i - TLAG
                if 0 <= j < NU:
                    s, h, k0, w, _, _ = units[j]
                    r = steps[s][2]
                    pe.wait_ge(w_ready, j + 1)
                    if j >= WB:
                        pe.wait_ge(wT_out, j - WB + 1)
                    for b in range(-(-w // P)):
                        kr = min(P, w - b * P)
                        last = nc.tensor.transpose(psW[j % WB][0:kr, b, 0:r], wb[j % NW][0:r, b * P:b * P + kr],
                                                   ident[0:r, 0:r])
                    last.then_inc(wT_ready, 1)


def recur(nc, tr, v_src, g_src, state_in, lower_bounds, onorm, state_outs, mix):
    tiles = [(SEQ, NEW, True)] + [(t * P, P, t > 0) for t in range(NT)]
    N = len(tiles)
    THR = 2.0 ** -50
    ctx = ExitStack()
    with ctx:
        S = Space(nc, ctx)
        W = H * P
        ident = S.sb("rc_ident", [P, P])
        masks = S.sb("rc_masks", [P, 8, P])
        keep = {r: S.sb(f"rc_keep{r}", [P, H * r]) for r in (P, NEW)}
        lraw, lexp, lsm, lb, oml, lbf = [S.sb("rc_" + x, [P, H]) for x in ("lraw", "lexp", "lsm", "lb", "oml", "lbf")]
        onr = S.sb("rc_onr", [P, P])
        minus_half = S.sb("rc_mhalf", [P, H])

        def pair(name, w=W):
            return [S.sb(f"rc_{name}{i}", [P, w]) for i in range(2)]

        q, sg, ks, v, g = (pair(x) for x in ("q", "sg", "ks", "v", "g"))
        k, f, a, b, la, lf, gs, e1, d2, e2, qh, kh = (
            pair(x) for x in ("k", "f", "a", "b", "la", "lf", "gs", "e1", "d2", "e2", "qh", "kh"))
        khn, gg, sqo, on = (pair(x) for x in ("khn", "gg", "sqo", "on"))
        so, rs = pair("so", H), pair("rs", H)
        NX = 3
        d, e, x = ([S.sb(f"rc_{z}{i}", [P, W]) for i in range(NX)] for z in ("d", "e", "x"))
        At = {n: S.sb(f"rc_At{n}", [P, H, P]) for n in range(3)}
        St = [S.sb(f"rc_S{i}", [P, H, P]) for i in range(3)]
        NA = 3
        psA = [S.ps(f"rc_psA{i}", [P, H, P]) for i in range(NA)]
        psK = S.ps("rc_psK", [P, H, P])
        psO = [S.ps(f"rc_psO{i}", [P, H, P]) for i in range(2)]
        psS = S.ps("rc_psS", [P, H, P])
        names = """init maskstep consts lexp_ready lchain k_ready f_step f_ready gg_ready ab_ready ln_ready
            lf_ready g_ready d_ready e_ready x_ready a_ready a_out d2_ready e12_ready qk_ready khT_ready khn_ready
            o_done s_done s_out sq_ready so_ready rsm_ready rs_ready osc_ready on_ready state_loaded""".split()
        s = {z: S.sem("rc_" + z) for z in names}
        loaded = [S.sem(f"rc_loaded{i}") for i in range(2)]
        stored = [S.sem(f"rc_stored{i}") for i in range(2)]
        state_stored = S.sem("rc_state_stored")

        def levels(n):
            r, out = tiles[n][1], []
            m = r // 2
            while m:
                out.append(m)
                m //= 2
            return out

        lev0 = [sum(len(levels(j)) for j in range(n)) for n in range(N + 1)]
        prod0 = [lev0[n] + n for n in range(N + 1)]

        def at(n):
            return At[2] if n == 0 else At[n % 2]

        def flat(buf, n):
            return buf[:, 0:H * tiles[n][1]]

        def heads(buf, n):
            return flat(buf, n).rearrange("p (h t) -> p h t", h=H)

        def blk(buf, n, m):
            return flat(buf, n).rearrange("p (b t) -> p b t", t=2 * m)

        block = ctx.enter_context(nc.Block())

        @block.sync
        def _(sp):
            sp.dma_start(lraw[:, :], lower_bounds.rearrange("(h p) -> p h", p=P), allow_slow_non_contiguous=True).then_inc(s["consts"], 16)
            sp.dma_start(onr[:, :], bcast_rows(onorm, P)).then_inc(s["consts"], 16)
            sp.dma_start(St[0][:, :, :], state_in.rearrange("h k v -> k h v")).then_inc(s["state_loaded"], 16)
            for n in range(N + 1):
                if n < N:
                    t0, r, _ = tiles[n]
                    if n >= 2:
                        sp.wait_ge(s["o_done"], n - 1)
                        sp.wait_ge(s["s_done"], n - 1)
                        sp.wait_ge(s["gg_ready"], n - 1)
                    for i, buf in enumerate((q, sg, ks)):
                        sp.dma_start(heads(buf[n % 2], n), tr[i, :, :, t0:t0 + r].rearrange("h p t -> p h t")
                                     ).then_inc(loaded[n % 2], 16)
                    sp.dma_start(v[n % 2][0:r, :], v_src(t0, r)).then_inc(loaded[n % 2], 16)
                    sp.dma_start(g[n % 2][0:r, :], g_src(t0, r)).then_inc(loaded[n % 2], 16)
                if n >= 1:
                    j = n - 1
                    t0, r, _ = tiles[j]
                    sp.wait_ge(s["on_ready"], j + 1)
                    sp.dma_start(mix[t0:t0 + r, :], on[j % 2][0:r, :]).then_inc(stored[j % 2], 16)
                    if j in (0, N - 1):
                        sp.wait_ge(s["s_out"], j + 1)
                        sp.dma_start(state_outs[0 if j else 1].rearrange("h k v -> k h v"),
                                     St[(j + 1) % 3][:, :, :]).then_inc(state_stored, 16)
            for i in range(2):
                sp.wait_ge(stored[i], 16 * len(range(i, N, 2)))
            sp.wait_ge(state_stored, 32)

        @block.gpsimd
        def _(pool):
            nc.gpsimd.memset(ident[:, :], 0.0)
            nc.gpsimd.memset(masks[:, :, :], 0.0)
            nc.gpsimd.memset(minus_half[:, :], -0.5)
            for i in range(3):
                nc.gpsimd.memset(At[i][:, :, :], 0.0)
            for r in (P, NEW):
                last = nc.gpsimd.memset(keep[r][:, :], 1.0)
            last.then_inc(s["maskstep"], 1)
            step = 1
            pool.wait_ge(s["maskstep"], step)
            for r in (P, NEW):
                nc.gpsimd.memset(keep[r][:, :].rearrange("p (h t) -> p h t", h=H)[:, :, 0:1], 0.0)
            for lv in range(7):
                m = 1 << lv
                nc.gpsimd.memset(masks[:, lv, :].rearrange("p (b t) -> p b t", t=2 * m)[:, :, m:2 * m], 1.0)
            nc.gpsimd.affine_select(out=masks[:, 7, :], in_=masks[:, 7, :], compare_op=ALU.not_equal, fill=1.0,
                                    base=0, pattern=[[-1, P]], channel_multiplier=1)
            nc.gpsimd.affine_select(out=ident[:, :], in_=ident[:, :], compare_op=ALU.not_equal, fill=1.0,
                                    base=0, pattern=[[-1, P]], channel_multiplier=1).then_inc(s["maskstep"], 1)
            step += 1
            for lv in range(7):
                m = 1 << lv
                mv = masks[:, lv, :].rearrange("p (b t) -> p b t", t=2 * m)
                for mult, base in ((1, 0), (-1, m - 1)):
                    pool.wait_ge(s["maskstep"], step)
                    nc.gpsimd.affine_select(out=mv, in_=mv, compare_op=ALU.is_ge, fill=0.0, base=base,
                                            pattern=[[-2 * m * mult, P // (2 * m)], [0, 2 * m]],
                                            channel_multiplier=mult).then_inc(s["maskstep"], 1)
                    step += 1
            pool.wait_ge(s["maskstep"], step)
            nc.gpsimd.memset(keep[P][0:1, 0:1], 0.0).then_inc(s["init"], 1)
            pool.wait_ge(s["lchain"], 6)

            def front(n):
                t0, r, _ = tiles[n]
                bb = n % 2
                pool.wait_ge(loaded[bb], 16 * 5 * (n // 2 + 1))
                if n >= 2:
                    pool.wait_ge(s["a_ready"], prod0[n - 1])
                    pool.wait_ge(s["on_ready"], n - 1)
                bc = [z[:, :].unsqueeze(2).to_broadcast([P, H, r]) for z in (oml, lbf)]
                nc.gpsimd.tensor_tensor(heads(f[bb], n), heads(sg[bb], n), bc[0], ALU.mult).then_inc(s["f_step"], 1)
                nc.gpsimd.tensor_tensor(heads(k[bb], n), heads(ks[bb], n), bc[0], ALU.mult).then_inc(s["k_ready"], 1)
                pool.wait_ge(s["f_step"], n + 1)
                nc.gpsimd.tensor_tensor(heads(f[bb], n), heads(f[bb], n), bc[1], ALU.add).then_inc(s["f_ready"], 1)
                nc.gpsimd.tensor_tensor(gg[bb][0:r, :].rearrange("p (h t) -> p h t", h=H),
                                        g[bb][0:r, :].rearrange("p (h t) -> p h t", h=H),
                                        onr[0:r, :].unsqueeze(1).to_broadcast([r, H, P]),
                                        ALU.mult).then_inc(s["gg_ready"], 1)

            front(0)
            pool.wait_ge(s["k_ready"], 1)
            for n in range(N):
                t0, r, _ = tiles[n]
                bb = n % 2
                if n >= 1:
                    pool.wait_ge(s["k_ready"], n + 1)
                for i, m in enumerate(levels(n)):
                    u = lev0[n] + i
                    pool.wait_ge(s["e_ready"], u + 1)
                    if u >= NX:
                        pn = max(j for j in range(N) if lev0[j] <= u - NX)
                        pool.wait_ge(s["a_ready"], prod0[pn] + (u - NX - lev0[pn]) + 1)
                    xv, ev = blk(x[u % NX], n, m), blk(e[u % NX], n, m)
                    nc.gpsimd.tensor_tensor(xv[:, :, 0:m], ev[:, :, 0:m], blk(k[bb], n, m)[:, :, 0:m], ALU.mult)
                    nc.gpsimd.tensor_tensor(xv[:, :, m:2 * m], ev[:, :, m:2 * m], blk(q[bb], n, m)[:, :, m:2 * m],
                                            ALU.mult).then_inc(s["x_ready"], 1)
                pool.wait_ge(s["e12_ready"], n + 1)
                if n >= 2:
                    pool.wait_ge(s["o_done"], n - 1)
                    pool.wait_ge(s["khT_ready"], n - 1)
                nc.gpsimd.tensor_tensor(flat(kh[bb], n), flat(k[bb], n), flat(e2[bb], n), ALU.mult)
                nc.gpsimd.tensor_tensor(flat(qh[bb], n), flat(q[bb], n), flat(e1[bb], n),
                                        ALU.mult).then_inc(s["qk_ready"], 1)
                if n + 1 < N:
                    front(n + 1)
                pool.wait_ge(s["so_ready"], n + 1)
                nc.gpsimd.tensor_scalar(rs[bb][0:r, :], so[bb][0:r, :], 1.0 / P, EPS, ALU.mult,
                                        ALU.add).then_inc(s["rsm_ready"], 1)
                pool.wait_ge(s["rsm_ready"], n + 1)
                nc.gpsimd.tensor_tensor(rs[bb][0:r, :], rs[bb][0:r, :], minus_half[0:r, :],
                                        ALU.pow).then_inc(s["rs_ready"], 1)

        @block.scalar
        def _(act):
            act.wait_ge(s["lchain"], 1)
            nc.scalar.activation(lexp[:, :], lsm[:, :], ACT.Exp).then_inc(s["lexp_ready"], 1)

            def front(n):
                bb = n % 2
                act.wait_ge(s["ab_ready"], n + 1)
                nc.scalar.activation(flat(la[bb], n), flat(a[bb], n), ACT.Ln)
                nc.scalar.activation(flat(lf[bb], n), flat(b[bb], n), ACT.Ln).then_inc(s["ln_ready"], 1)

            front(0)
            for n in range(N):
                r = tiles[n][1]
                bb = n % 2
                for i, m in enumerate(levels(n)):
                    u = lev0[n] + i
                    act.wait_ge(s["d_ready"], u + 1)
                    if u >= NX:
                        act.wait_ge(s["x_ready"], u - NX + 1)
                    nc.scalar.activation(flat(e[u % NX], n), flat(d[u % NX], n), ACT.Exp).then_inc(s["e_ready"], 1)
                act.wait_ge(s["d2_ready"], n + 1)
                if n >= 2:
                    act.wait_ge(s["s_out"], n - 1)
                nc.scalar.activation(flat(e1[bb], n), flat(gs[bb], n), ACT.Exp)
                nc.scalar.activation(flat(e2[bb], n), flat(d2[bb], n), ACT.Exp).then_inc(s["e12_ready"], 1)
                if n + 1 < N:
                    front(n + 1)
                act.wait_ge(s["khT_ready"], n + 1)
                if n >= 2:
                    act.wait_ge(s["s_done"], n - 1)
                nc.scalar.activation(khn[bb][0:r, :].rearrange("p (h t) -> p h t", h=H), psK[0:r, :, :],
                                     ACT.Copy).then_inc(s["khn_ready"], 1)
                act.wait_ge(s["o_done"], n + 1)
                nc.scalar.activation(sqo[bb][0:r, :].rearrange("p (h t) -> p h t", h=H), psO[bb][0:r, :, :],
                                     ACT.Square).then_inc(s["sq_ready"], 1)

        @block.vector
        def _(dve):
            dve.wait_ge(s["consts"], 32)
            nc.vector.tensor_tensor(lsm[:, :], lraw[:, :], lraw[:, :], ALU.subtract).then_inc(s["lchain"], 1)
            dve.wait_ge(s["lexp_ready"], 1)
            nc.vector.reciprocal(lb[:, :], lexp[:, :]).then_inc(s["lchain"], 1)
            dve.wait_ge(s["lchain"], 2)
            nc.vector.tensor_tensor(lsm[:, :], lexp[:, :], lb[:, :], ALU.mult).then_inc(s["lchain"], 1)
            dve.wait_ge(s["lchain"], 3)
            nc.vector.tensor_tensor(lb[:, :], lsm[:, :], lsm[:, :], ALU.subtract).then_inc(s["lchain"], 1)
            dve.wait_ge(s["lchain"], 4)
            nc.vector.tensor_scalar(oml[:, :], lb[:, :], -1.0, 1.0, ALU.mult, ALU.add).then_inc(s["lchain"], 1)
            nc.vector.tensor_scalar(lbf[:, :], lb[:, :], 1e-30, None, ALU.max).then_inc(s["lchain"], 1)
            dve.wait_ge(s["init"], 1)

            def front(n):
                r, bb = tiles[n][1], n % 2
                dve.wait_ge(s["f_ready"], n + 1)
                nc.vector.tensor_scalar(flat(a[bb], n), flat(f[bb], n), THR, None, ALU.max)
                nc.vector.tensor_scalar(flat(b[bb], n), flat(f[bb], n), THR, 1.0 / THR, ALU.min,
                                        ALU.mult).then_inc(s["ab_ready"], 1)
                dve.wait_ge(s["ln_ready"], n + 1)
                nc.vector.tensor_tensor(flat(lf[bb], n), flat(lf[bb], n), flat(la[bb], n),
                                        ALU.add).then_inc(s["lf_ready"], 1)
                dve.wait_ge(s["lf_ready"], n + 1)
                nc.vector.tensor_tensor_scan(out=flat(gs[bb], n), data0=keep[r][:, :], data1=flat(lf[bb], n),
                                             initial=0.0, op0=ALU.mult, op1=ALU.add).then_inc(s["g_ready"], 1)

            def take(n, i):
                r = tiles[n][1]
                p = prod0[n] + i
                lv = 7 if i == len(levels(n)) else levels(n)[i].bit_length() - 1
                dve.wait_ge(s["a_ready"], p + 1)
                if i == 0 and n >= 3:
                    dve.wait_ge(s["o_done"], n - 1)
                if p >= 1:
                    dve.wait_ge(s["a_out"], p)
                nc.vector.copy_predicated(at(n)[0:r, :, 0:r],
                                          masks[0:r, lv:lv + 1, 0:r].to_broadcast([r, H, r]).bitcast(I32),
                                          psA[p % NA][0:r, :, 0:r]).then_inc(s["a_out"], 1)

            front(0)
            for n in range(N):
                r, bb = tiles[n][1], n % 2
                dve.wait_ge(s["g_ready"], n + 1)
                lv = levels(n)
                for i, m in enumerate(lv):
                    u = lev0[n] + i
                    if u >= NX:
                        dve.wait_ge(s["e_ready"], u - NX + 1)
                    dv, gv = blk(d[u % NX], n, m), blk(gs[bb], n, m)
                    nb = H * r // (2 * m)
                    mid = gv[:, :, m - 1:m].to_broadcast([P, nb, m])
                    nc.vector.tensor_tensor(dv[:, :, 0:m], mid, gv[:, :, 0:m], ALU.subtract)
                    nc.vector.tensor_tensor(dv[:, :, m:2 * m], gv[:, :, m:2 * m], mid,
                                            ALU.subtract).then_inc(s["d_ready"], 1)
                    if i == 2:
                        gh = heads(gs[bb], n)
                        if n >= 2:
                            dve.wait_ge(s["e12_ready"], n - 1)
                        nc.vector.tensor_tensor(heads(d2[bb], n), gh[:, :, r - 1:r].to_broadcast([P, H, r]), gh,
                                                ALU.subtract).then_inc(s["d2_ready"], 1)
                    if i >= 3:
                        take(n, i - 3)
                for i in range(len(lv) - 3, len(lv) + 1):
                    take(n, i)
                if n + 1 < N:
                    front(n + 1)
                dve.wait_ge(s["s_done"], n + 1)
                new, old = St[(n + 1) % 3], St[n % 3]
                if n == 3:
                    dve.wait_ge(state_stored, 16)
                if n >= 3:
                    dve.wait_ge(s["o_done"], n - 1)
                if tiles[n][2]:
                    if n >= 2:
                        dve.wait_ge(s["s_out"], n)
                    for h in range(H):
                        last = nc.vector.scalar_tensor_tensor(
                            out=new[:, h, :], in0=old[:, h, :], scalar=heads(e1[bb], n)[:, h, r - 1:r],
                            in1=psS[:, h, :], op0=ALU.mult, op1=ALU.add)
                else:
                    last = nc.vector.tensor_copy(new[:, :, :], psS[:, :, :])
                last.then_inc(s["s_out"], 1)
                dve.wait_ge(s["sq_ready"], n + 1)
                nc.vector.tensor_reduce(so[bb][0:r, :], sqo[bb][0:r, :].rearrange("p (h t) -> p h t", h=H),
                                        axis=AX.X, op=ALU.add).then_inc(s["so_ready"], 1)
                dve.wait_ge(s["rs_ready"], n + 1)
                if n >= 2:
                    dve.wait_ge(stored[bb], 16 * (n // 2))
                nc.vector.tensor_tensor(on[bb][0:r, :].rearrange("p (h t) -> p h t", h=H), psO[bb][0:r, :, :],
                                        rs[bb][0:r, :].unsqueeze(2).to_broadcast([r, H, P]),
                                        ALU.mult).then_inc(s["osc_ready"], 1)
                dve.wait_ge(s["osc_ready"], n + 1)
                nc.vector.tensor_tensor(on[bb][0:r, :], on[bb][0:r, :], gg[bb][0:r, :],
                                        ALU.mult).then_inc(s["on_ready"], 1)

        @block.tensor
        def _(pe):
            pe.wait_ge(s["init"], 1)
            pe.wait_ge(s["state_loaded"], 16)
            for n in range(N):
                t0, r, before = tiles[n]
                bb = n % 2
                lv = levels(n)
                for i in range(len(lv) + 1):
                    p = prod0[n] + i
                    if i < len(lv):
                        u = lev0[n] + i
                        pe.wait_ge(s["x_ready"], u + 1)
                        lhs = rhs = heads(x[u % NX], n)
                    else:
                        lhs, rhs = heads(k[bb], n), heads(q[bb], n)
                    if p >= NA:
                        pe.wait_ge(s["a_out"], p - NA + 1)
                    for h in range(H):
                        last = nc.tensor.matmul(psA[p % NA][0:r, h, 0:r], lhs[:, h, :], rhs[:, h, :],
                                                start=True, stop=True)
                    last.then_inc(s["a_ready"], 1)
                pe.wait_ge(s["qk_ready"], n + 1)
                if n >= 1:
                    pe.wait_ge(s["khn_ready"], n)
                for h in range(H):
                    last = nc.tensor.transpose(psK[0:r, h, :], heads(kh[bb], n)[:, h, :], ident[:, :])
                last.then_inc(s["khT_ready"], 1)
                pe.wait_ge(s["khn_ready"], n + 1)
                if n >= 1:
                    pe.wait_ge(s["s_out"], n)
                for h in range(H):
                    last = nc.tensor.matmul(psS[:, h, :], khn[bb][0:r, h * P:(h + 1) * P],
                                            v[bb][0:r, h * P:(h + 1) * P], start=True, stop=True)
                last.then_inc(s["s_done"], 1)
                pe.wait_ge(s["a_out"], prod0[n + 1])
                if n >= 2:
                    pe.wait_ge(s["on_ready"], n - 1)
                for h in range(H):
                    last = nc.tensor.matmul(psO[bb][0:r, h, :], at(n)[0:r, h, 0:r], v[bb][0:r, h * P:(h + 1) * P],
                                            start=True, stop=not before)
                    if before:
                        last = nc.tensor.matmul(psO[bb][0:r, h, :], heads(qh[bb], n)[:, h, :], St[n % 3][:, h, :],
                                                start=False, stop=True)
                last.then_inc(s["o_done"], 1)


def merge_and_ffn(nc, mix, x, w_o, norm_ffn, w_up, w_down, y):
    FP = 2
    NP = DFF // (FP * P)
    PIECE = FP * D
    NPC = KD // FP + 2 * NP
    HT = max(sum(r for _, r in th) for th in THIRDS)
    NTH = len(THIRDS)
    n0 = [sum(len(z) for z in THIRDS[:t]) for t in range(NTH)]
    ctx = ExitStack()
    with ctx:
        S = Space(nc, ctx)
        ident = S.sb("mf_ident", [P, P])
        grow = S.sb("mf_grow", [P, D])
        mhalf = S.sb("mf_mhalf", [P, 1])
        nat = [S.sb(f"mf_nat{i}", [P, D]) for i in range(2)]
        xin = [S.sb(f"mf_xin{i}", [P, D]) for i in range(2)]
        hs = [S.sb(f"mf_hs{i}", [P, D]) for i in range(2)]
        ss = S.sb("mf_ss", [P, len(TILES)])
        rstd = S.sb("mf_rstd", [P, len(TILES)])
        acc = S.sb("mf_acc", [P, max(len(z) for z in THIRDS), D])
        xhi = S.sb("mf_xhi", [P, KD, HT], F32R)
        xlo = S.sb("mf_xlo", [P, KD, HT], F32R)
        st = [S.sb(f"mf_st{i}", [P, PIECE]) for i in range(2)]
        whi = [S.sb(f"mf_whi{i}", [P, PIECE], F32R) for i in range(4)]
        wlo = [S.sb(f"mf_wlo{i}", [P, PIECE], F32R) for i in range(4)]
        uhi = S.sb("mf_uhi", [P, 2 * FP, HT], F32R)
        ulo = S.sb("mf_ulo", [P, 2 * FP, HT], F32R)
        rl = [hs[i][:, 0:HT // 2] for i in range(2)]
        sq = [hs[i][:, HT // 2:HT] for i in range(2)]
        psT = [S.ps(f"mf_psT{i}", [P, KD, P]) for i in range(2)]
        psO = [S.ps(f"mf_psO{i}", [P, D]) for i in range(2)]
        names = """init consts t_ready hi_ready lo_ready whi_ready wlo_ready o_done o_out squared mean_ready
            rstd_ready hs_ready up_done relu_ready uhi_ready sq_ready ulo_ready""".split()
        s = {z: S.sem("mf_" + z) for z in names}
        nat_loaded = [S.sem(f"mf_nat_loaded{i}") for i in range(2)]
        x_loaded = [S.sem(f"mf_x_loaded{i}") for i in range(2)]
        w_loaded = [S.sem(f"mf_w_loaded{i}") for i in range(2)]
        stored = S.sem("mf_stored")

        def t_index(t, i, second):
            return 2 * n0[t] + (len(THIRDS[t]) if second else 0) + i

        def o_index(t, i, p):
            return (NP + 1) * n0[t] + (p + 1) * len(THIRDS[t]) + i

        def up_index(t, f, b):
            return (t * DFF // P + f) * 2 + b

        def piece(t, what, p):
            k = p if what == "o" else KD // FP + 2 * p + (what == "d")
            return t * NPC + k

        def wbuf(what, p):
            return p if what == "o" else p % 2 + 2 * (what == "d")

        def piece_src(what, p):
            if what == "u":
                return w_up[:, p * FP * P:(p + 1) * FP * P].rearrange("(k p) n -> p k n", p=P)
            w = w_o if what == "o" else w_down
            return w[p * FP * P:(p + 1) * FP * P, :].rearrange("(k p) n -> p k n", p=P)

        def wait_wbuf_free(eng, t, what, p):
            if what == "o":
                if t:
                    eng.wait_ge(s["o_done"], o_index(t, 0, -1))
            elif p < 2:
                eng.wait_ge(s["o_done"], o_index(t, 0, 0))
            elif what == "u":
                eng.wait_ge(s["up_done"], up_index(t, FP * (p - 1), 0))
            else:
                eng.wait_ge(s["o_done"], o_index(t, 0, p - 1))

        order = [("o", p) for p in range(KD // FP)]
        for p in range(NP):
            order += [("u", p), ("d", p)]

        def split_plan(p):
            out = []
            if p + 2 < NP:
                out.append(("u", p + 2))
            if p + 1 < NP:
                out.append(("d", p + 1))
            return sorted(out, key=order.index)

        block = ctx.enter_context(nc.Block())

        @block.sync
        def _(sp):
            sp.dma_start(grow[:, :], bcast_rows(norm_ffn, P)).then_inc(s["consts"], 16)

            def load_piece(t, what, p):
                m = piece(t, what, p)
                if m >= 2:
                    sp.wait_ge(s["whi_ready"], m - 1)
                    sp.wait_ge(s["wlo_ready"], m - 1)
                src = piece_src(what, p)
                sp.dma_start(st[m % 2][:, :].rearrange("p (k n) -> p k n", k=src.shape[1]), src
                             ).then_inc(w_loaded[m % 2], 16)

            for t, tiles in enumerate(THIRDS):
                for i, (t0, r) in enumerate(tiles):
                    n = n0[t] + i
                    if i >= 2 or t:
                        sp.wait_ge(s["t_ready"], t_index(t, i - 2, False) + 1 if i >= 2 else t_index(t, 0, False))
                    sp.dma_start(nat[n % 2][0:r, :], mix[t0:t0 + r, :]).then_inc(nat_loaded[n % 2], 16)
                    if 1 <= i <= KD // FP:
                        load_piece(t, "o", i - 1)
                for i, (t0, r) in enumerate(tiles):
                    n = n0[t] + i
                    if n >= 2:
                        sp.wait_ge(s["o_out"], o_index(t, i - 2, -1) + 1 if i >= 2 else o_index(t, 0, -1))
                    sp.dma_start(xin[n % 2][0:r, :], x(t0, r)).then_inc(x_loaded[n % 2], 16)
                for what, p in order[KD // FP:]:
                    load_piece(t, what, p)
                for i, (t0, r) in enumerate(tiles):
                    sp.wait_ge(s["o_out"], o_index(t, i, NP - 1) + 1)
                    sp.dma_start(y(t0, r), acc[0:r, i, :]).then_inc(stored, 16)
            sp.wait_ge(stored, 16 * len(TILES))

        @block.gpsimd
        def _(pool):
            nc.gpsimd.memset(ident[:, :], 0.0).then_inc(s["init"], 1)
            nc.gpsimd.memset(mhalf[:, :], -0.5).then_inc(s["init"], 1)
            pool.wait_ge(s["init"], 2)
            nc.gpsimd.affine_select(out=ident[:, :], in_=ident[:, :], compare_op=ALU.not_equal, fill=1.0,
                                    base=0, pattern=[[-1, P]], channel_multiplier=1).then_inc(s["init"], 1)
            for n, (t0, r) in enumerate(TILES):
                pool.wait_ge(s["squared"], n + 1)
                nc.gpsimd.tensor_scalar(rstd[0:r, n:n + 1], ss[0:r, n:n + 1], 1.0 / D, EPS,
                                        ALU.mult, ALU.add).then_inc(s["mean_ready"], 1)
                pool.wait_ge(s["mean_ready"], n + 1)
                nc.gpsimd.tensor_tensor(rstd[0:r, n:n + 1], rstd[0:r, n:n + 1], mhalf[0:r, 0:1],
                                        ALU.pow).then_inc(s["rstd_ready"], 1)

        @block.scalar
        def _(act):
            def split(t, what, p):
                m = piece(t, what, p)
                act.wait_ge(w_loaded[m % 2], 16 * (m // 2 + 1))
                wait_wbuf_free(act, t, what, p)
                nc.scalar.activation(whi[wbuf(what, p)][:, :], st[m % 2][:, :], ACT.Copy
                                     ).then_inc(s["whi_ready"], 1)

            for t, tiles in enumerate(THIRDS):
                nt, base = len(tiles), tiles[0][0]
                bl = blocks_of(sum(r for _, r in tiles))

                def hi(i, second):
                    t0, r = tiles[i]
                    k = t_index(t, i, second)
                    act.wait_ge(s["t_ready"], k + 1)
                    c = slice(t0 - base, t0 - base + r)
                    nc.scalar.activation(xhi[:, :, c], psT[k % 2][:, :, 0:r], ACT.Copy).then_inc(s["hi_ready"], 1)

                def square(i):
                    n, r = n0[t] + i, tiles[i][1]
                    act.wait_ge(s["o_out"], o_index(t, i, -1) + 1)
                    if i >= 2 or t:
                        act.wait_ge(s["t_ready"], t_index(t, i - 2, True) + 1 if i >= 2 else
                                    t_index(t - 1, len(THIRDS[t - 1]) - 1, True) + 1)
                    nc.scalar.activation(hs[n % 2][0:r, :], acc[0:r, i, :], ACT.Square,
                                         accum_out=ss[0:r, n:n + 1]).then_inc(s["squared"], 1)

                if t:
                    act.wait_ge(s["up_done"], up_index(t, 0, 0))
                for i in range(nt):
                    hi(i, False)
                    if 1 <= i <= KD // FP:
                        split(t, "o", i - 1)
                for i in range(nt):
                    square(i)
                    if i >= 1:
                        hi(i - 1, True)
                hi(nt - 1, True)
                split(t, "u", 0)
                for p in range(-1, NP):
                    for what, pp in split_plan(p):
                        split(t, what, pp)
                    if p + 1 < NP:
                        for f in range(FP * (p + 1), FP * (p + 2)):
                            for b, (c0, cn) in enumerate(bl):
                                k = up_index(t, f, b)
                                ps = psT[(k % 4) // 2][:, :, :].rearrange("p k n -> p (k n)")[
                                    :, (k % 2) * 512:(k % 2) * 512 + cn]
                                act.wait_ge(s["up_done"], k + 1)
                                if k >= 2:
                                    act.wait_ge(s["sq_ready"], k - 1)
                                nc.scalar.activation(rl[k % 2][:, 0:cn], ps, ACT.Relu).then_inc(s["relu_ready"], 1)
                                act.wait_ge(s["relu_ready"], k + 1)
                                if b == 0 and p >= 1:
                                    act.wait_ge(s["o_done"], o_index(t, 0, p))
                                nc.scalar.activation(uhi[:, f % (2 * FP), c0:c0 + cn], rl[k % 2][:, 0:cn],
                                                     ACT.Square).then_inc(s["uhi_ready"], 1)

        @block.vector
        def _(dve):
            def split(t, what, p):
                m = piece(t, what, p)
                dve.wait_ge(s["whi_ready"], m + 1)
                wait_wbuf_free(dve, t, what, p)
                b = wbuf(what, p)
                nc.vector.tensor_tensor(wlo[b][:, :], st[m % 2][:, :], whi[b][:, :].bitcast(F32),
                                        ALU.subtract).then_inc(s["wlo_ready"], 1)

            dve.wait_ge(s["consts"], 16)
            for t, tiles in enumerate(THIRDS):
                nt, base = len(tiles), tiles[0][0]
                bl = blocks_of(sum(r for _, r in tiles))

                def lo(i, second):
                    t0, r = tiles[i]
                    k = t_index(t, i, second)
                    dve.wait_ge(s["hi_ready"], k + 1)
                    c = slice(t0 - base, t0 - base + r)
                    nc.vector.tensor_tensor(xlo[:, :, c], psT[k % 2][:, :, 0:r], xhi[:, :, c].bitcast(F32),
                                            ALU.subtract).then_inc(s["lo_ready"], 1)

                def add_x(i):
                    n, r, k = n0[t] + i, tiles[i][1], o_index(t, i, -1)
                    dve.wait_ge(s["o_done"], k + 1)
                    dve.wait_ge(x_loaded[n % 2], 16 * (n // 2 + 1))
                    if t:
                        dve.wait_ge(stored, 16 * n0[t])
                    nc.vector.tensor_tensor(acc[0:r, i, :], psO[k % 2][0:r, :], xin[n % 2][0:r, :],
                                            ALU.add).then_inc(s["o_out"], 1)

                def scale(i):
                    n, r = n0[t] + i, tiles[i][1]
                    dve.wait_ge(s["rstd_ready"], n + 1)
                    nc.vector.scalar_tensor_tensor(out=hs[n % 2][0:r, :], in0=acc[0:r, i, :],
                                                   scalar=rstd[0:r, n:n + 1], in1=grow[0:r, :],
                                                   op0=ALU.mult, op1=ALU.mult).then_inc(s["hs_ready"], 1)

                for i in range(nt):
                    lo(i, False)
                    if 1 <= i <= KD // FP:
                        split(t, "o", i - 1)
                for i in range(nt):
                    add_x(i)
                    scale(i)
                    if i >= 1:
                        lo(i - 1, True)
                lo(nt - 1, True)
                split(t, "u", 0)
                for p in range(-1, NP):
                    for what, pp in split_plan(p):
                        split(t, what, pp)
                    if p + 1 < NP:
                        for f in range(FP * (p + 1), FP * (p + 2)):
                            for b, (c0, cn) in enumerate(bl):
                                k = up_index(t, f, b)
                                ps = psT[(k % 4) // 2][:, :, :].rearrange("p k n -> p (k n)")[
                                    :, (k % 2) * 512:(k % 2) * 512 + cn]
                                dve.wait_ge(s["relu_ready"], k + 1)
                                nc.vector.tensor_tensor(sq[k % 2][:, 0:cn], ps, rl[k % 2][:, 0:cn],
                                                        ALU.mult).then_inc(s["sq_ready"], 1)
                                dve.wait_ge(s["sq_ready"], k + 1)
                                dve.wait_ge(s["uhi_ready"], k + 1)
                                nc.vector.tensor_tensor(ulo[:, f % (2 * FP), c0:c0 + cn], sq[k % 2][:, 0:cn],
                                                        uhi[:, f % (2 * FP), c0:c0 + cn].bitcast(F32),
                                                        ALU.subtract).then_inc(s["ulo_ready"], 1)
                    if p >= 0:
                        for i, (t0, r) in enumerate(tiles):
                            k = o_index(t, i, p)
                            dve.wait_ge(s["o_done"], k + 1)
                            dve.wait_ge(s["o_out"], k)
                            nc.vector.tensor_tensor(acc[0:r, i, :], psO[k % 2][0:r, :], acc[0:r, i, :],
                                                    ALU.add).then_inc(s["o_out"], 1)

        @block.tensor
        def _(pe):
            pe.wait_ge(s["init"], 3)
            for t, tiles in enumerate(THIRDS):
                nt, base = len(tiles), tiles[0][0]
                bl = blocks_of(sum(r for _, r in tiles))

                def turn(i, second):
                    t0, r = tiles[i]
                    n, k = n0[t] + i, t_index(t, i, second)
                    if second:
                        pe.wait_ge(s["hs_ready"], n + 1)
                    else:
                        pe.wait_ge(nat_loaded[n % 2], 16 * (n // 2 + 1))
                    if k >= 2:
                        pe.wait_ge(s["lo_ready"], k - 1)
                    if t and i == 0 and not second:
                        pe.wait_ge(s["sq_ready"], up_index(t, 0, 0))
                    src = (hs if second else nat)[n % 2]
                    for j in range(KD):
                        last = nc.tensor.transpose(psT[k % 2][:, j, 0:r], src[0:r, j * P:(j + 1) * P],
                                                   ident[0:r, 0:r])
                    last.then_inc(s["t_ready"], 1)

                def product(k, r, steps):
                    if k >= 2:
                        pe.wait_ge(s["o_out"], k - 1)
                    for half in range(2):
                        c = slice(half * 512, half * 512 + 512)
                        for j, (xa, wa) in enumerate(steps):
                            last = nc.tensor.matmul(psO[k % 2][0:r, c], xa, wa[:, c], start=j == 0,
                                                    stop=j == len(steps) - 1)
                    last.then_inc(s["o_done"], 1)

                def out_proj(i):
                    t0, r = tiles[i]
                    c = slice(t0 - base, t0 - base + r)
                    steps = []
                    for j in range(KD):
                        b, w0 = j // FP, (j % FP) * D
                        for xa, wa in ((xhi, whi), (xhi, wlo), (xlo, whi)):
                            steps.append((xa[:, j, c], wa[b][:, w0:w0 + D]))
                    product(o_index(t, i, -1), r, steps)

                for i in range(nt):
                    turn(i, False)
                pe.wait_ge(s["wlo_ready"], piece(t, "o", KD // FP - 1) + 1)
                pe.wait_ge(s["lo_ready"], t_index(t, nt - 1, False) + 1)
                for i in range(nt):
                    out_proj(i)
                    if i >= 1:
                        turn(i - 1, True)
                turn(nt - 1, True)
                pe.wait_ge(s["lo_ready"], t_index(t, nt - 1, True) + 1)
                for p in range(-1, NP):
                    if p + 1 < NP:
                        pe.wait_ge(s["wlo_ready"], piece(t, "u", p + 1) + 1)
                        b4 = wbuf("u", p + 1)
                        for f in range(FP * (p + 1), FP * (p + 2)):
                            for b, (c0, cn) in enumerate(bl):
                                k = up_index(t, f, b)
                                ps = psT[(k % 4) // 2][:, :, :].rearrange("p k n -> p (k n)")[
                                    :, (k % 2) * 512:(k % 2) * 512 + cn]
                                if k >= 4:
                                    pe.wait_ge(s["sq_ready"], k - 3)
                                for j in range(KD):
                                    w0 = j * FP * P + (f % FP) * P
                                    for q, (wa, xa) in enumerate(((whi, xhi), (whi, xlo), (wlo, xhi))):
                                        last = nc.tensor.matmul(ps, wa[b4][:, w0:w0 + P], xa[:, j, c0:c0 + cn],
                                                                start=j == 0 and q == 0,
                                                                stop=j == KD - 1 and q == 2)
                                last.then_inc(s["up_done"], 1)
                    if p >= 0:
                        pe.wait_ge(s["wlo_ready"], piece(t, "d", p) + 1)
                        pe.wait_ge(s["ulo_ready"], up_index(t, FP * (p + 1), 0))
                        bd = wbuf("d", p)
                        for i, (t0, r) in enumerate(tiles):
                            c = slice(t0 - base, t0 - base + r)
                            steps = []
                            for j in range(FP):
                                f = (FP * p + j) % (2 * FP)
                                for ua, wa in ((uhi, whi), (uhi, wlo), (ulo, whi)):
                                    steps.append((ua[:, f, c], wa[bd][:, j * D:(j + 1) * D]))
                            product(o_index(t, i, p), r, steps)


def build(nc, a, outs):
    (yp, ys, akp, avp, bkp, bvp, csp, aks, avs, bks, bvs, css) = outs

    def rows(ap):
        return ap[0, 0].rearrange("t h d -> t (h d)")

    proj = nc.dram_tensor("scratch_proj", [NG, T, G], F32).ap()
    tr = nc.dram_tensor("scratch_tr", [3, H, P, T], F32).ap()
    mix = nc.dram_tensor("scratch_mix", [T, D], F32).ap()
    line = nc.dram_tensor("scratch_line", [H, NLINE], F32).ap()

    def x(t0, r):
        return a["x_prompt"][0, t0:t0 + r, :] if t0 < SEQ else a["x_sample"][0, 0:r, :]

    def y(t0, r):
        return yp[0, t0:t0 + r, :] if t0 < SEQ else ys[0, 0:r, :]

    gains = [a[n][0] for n in ("qnorm_a", "knorm_a", "qnorm_b", "knorm_b")]
    natural = {"akp": akp, "avp": avp, "bkp": bkp, "bvp": bvp, "aks": aks, "avs": avs, "bks": bks, "bvs": bvs}
    project(nc, x, a["norm_mix"][0], a["w_in"][0], gains, proj, tr, {n: rows(z) for n, z in natural.items()})

    def source(group, col, cache=None):
        def at(seq, t0, r):
            if seq == "s" and t0 < PAST:
                return rows(cache)[t0:t0 + r, :]
            t = SEQ if seq == "s" else t0
            return proj[group, t:t + r, col:col + WH]
        return at

    def by_head(at):
        return lambda seq, t0, r: at(seq, t0, r).rearrange("t (h d) -> t h d", h=H)

    attend(nc, "A", by_head(source(QKA, 0)), by_head(source(QKA, WH, a["cache_a_k"])),
           source(VQ, 0, a["cache_a_v"]), None, mix[:, 0:WH])
    attend(nc, "B", by_head(source(VQ, WH)), by_head(source(KV, 0, a["cache_b_k"])),
           source(KV, WH, a["cache_b_v"]), (a["rel_bias_b"][0], line), mix[:, WH:2 * WH])
    recur(nc, tr, lambda t0, r: proj[IC, t0:t0 + r, :], lambda t0, r: proj[GC, t0:t0 + r, :],
          a["state_c"][0, 0], a["lower_bounds"][0], a["onorm_c"][0], [csp[0, 0], css[0, 0]], mix[:, 2 * WH:D])
    merge_and_ffn(nc, mix, x, a["w_o"][0], a["norm_ffn"][0], a["w_up"][0], a["w_down"][0], y)


_INS = ["x_prompt", "x_sample", "cache_a_k", "cache_a_v", "cache_b_k", "cache_b_v", "state_c", "norm_mix", "w_in",
        "qnorm_a", "knorm_a", "qnorm_b", "knorm_b", "rel_bias_b", "lower_bounds", "onorm_c", "w_o", "norm_ffn",
        "w_up", "w_down"]
_KP, _KB, _KS = (1, 1, SEQ, H, DH), (1, 1, PREV * CHUNK, H, DH), (1, 1, NEW, H, DH)
_ST = (1, 1, H, P, P)
_OUTS = [(1, SEQ, D), (1, NEW, D), _KP, _KP, _KB, _KB, _ST, _KS, _KS, _KS, _KS, _ST]


def kernel(**inputs):
    import numpy as np
    import concourse.bacc as bacc
    from concourse.bass_utils import run_bass_kernel_spmd

    nc = bacc.Bacc("TRN2", target_bir_lowering=False, num_devices=1)
    arrays, a = {}, {}
    for name in _INS:
        v = np.ascontiguousarray(inputs[name])
        arrays["in_" + name] = v
        a[name] = nc.dram_tensor("in_" + name, v.shape, mybir.dt.from_np(v.dtype), kind="ExternalInput").ap()
    outs = [nc.dram_tensor(f"out_{i}", shape, F32, kind="ExternalOutput").ap() for i, shape in enumerate(_OUTS)]
    build(nc, a, outs)
    r = run_bass_kernel_spmd(nc, [arrays], core_ids=[0])
    return tuple(r.results[0][f"out_{i}"] for i in range(len(_OUTS)))
```

```python
from contextlib import ExitStack

import concourse.bass as bass
from concourse import mybir

F32 = mybir.dt.float32
F32R = mybir.dt.float32r
I32 = mybir.dt.int32
ALU = mybir.AluOpType
ACT = mybir.ActivationFunctionType
AX = mybir.AxisListType

P = 128
D = 1024
KD = D // P
SEQ, NEW, PAST = 2048, 32, 512
T = SEQ + NEW
NT = SEQ // P
DH, H = 64, 4
WH = H * DH
G = 512
NG = 7
DFF = 4 * D
CHUNK, PREV = 64, 8
CLIP = 128
BW = PREV * CHUNK + P
NLINE = BW + P - 1
EPS = 1e-6
NEG = -1e30
TILES = [(t * P, P) for t in range(NT)] + [(SEQ, NEW)]
HALVES = [TILES[:NT // 2], TILES[NT // 2:]]
THIRDS = [TILES[0:6], TILES[6:12], TILES[12:]]
QKA, VQ, KV, QC, FC, IC, GC = range(NG)


def blocks_of(n):
    k = -(-n // 512)
    while n % k:
        k += 1
    return [(i * (n // k), n // k) for i in range(k)]


class Space:

    def __init__(self, nc, ctx):
        self.nc, self.ctx = nc, ctx

    def sb(self, name, shape, dt=F32):
        return self.ctx.enter_context(self.nc.sbuf_tensor(name, shape, dt))

    def ps(self, name, shape):
        return self.ctx.enter_context(self.nc.psum_tensor(name, shape, F32))

    def sem(self, name):
        return self.ctx.enter_context(self.nc.semaphore(name))


def bcast_rows(ap, rows):
    return ap.rearrange("(a n) -> a n", a=1).to_broadcast([rows, ap.shape[0]])


def project(nc, x, norm_mix, w_in, gains, lower_bounds, onorm, proj, tr, outs):
    ctx = ExitStack()
    with ctx:
        S = Space(nc, ctx)
        ident = S.sb("pj_ident", [P, P])
        grow = S.sb("pj_grow", [P, D])
        gain = S.sb("pj_gain", [P, 4, DH])
        minus_half = S.sb("pj_mhalf", [P, 8])
        xin = [S.sb(f"pj_xin{i}", [P, D]) for i in range(2)]
        xs = [S.sb(f"pj_xs{i}", [P, D]) for i in range(2)]
        ss = S.sb("pj_ss", [P, len(TILES)])
        rstd = S.sb("pj_rstd", [P, len(TILES)])
        HT = max(sum(r for _, r in h) for h in HALVES)
        xhi = S.sb("pj_xhi", [P, KD, HT], F32R)
        xlo = S.sb("pj_xlo", [P, KD, HT], F32R)
        wst = S.sb("pj_wst", [P, KD, G])
        whi = [S.sb(f"pj_whi{i}", [P, KD, G], F32R) for i in range(2)]
        wlo = [S.sb(f"pj_wlo{i}", [P, KD, G], F32R) for i in range(2)]
        NO = 4
        sq = [S.sb(f"pj_sq{i}", [P, G]) for i in range(NO)]
        ob = [S.sb(f"pj_ob{i}", [P, G]) for i in range(NO)]
        hs = [S.sb(f"pj_hs{i}", [P, 8]) for i in range(NO)]
        hr = [S.sb(f"pj_hr{i}", [P, 8]) for i in range(NO)]
        psT = [S.ps(f"pj_psT{i}", [P, KD, P]) for i in range(2)]
        psO = [S.ps(f"pj_psO{i}", [P, G]) for i in range(NO)]
        lraw, lexp, lsm, lb, oml, lbf = [S.sb("pj_" + z, [P, H]) for z in ("lraw", "lexp", "lsm", "lb", "oml", "lbf")]
        onr = S.sb("pj_onr", [P, P])
        lexp_ready = S.sem("pj_lexp_ready")
        lchain = S.sem("pj_lchain")
        gated = S.sem("pj_gated")
        consts = S.sem("pj_consts")
        more_consts = S.sem("pj_more_consts")
        ident_step = S.sem("pj_ident_step")
        x_loaded = [S.sem(f"pj_x_loaded{i}") for i in range(2)]
        squared = S.sem("pj_squared")
        mean_ready = S.sem("pj_mean_ready")
        rstd_ready = S.sem("pj_rstd_ready")
        xs_ready = S.sem("pj_xs_ready")
        xT_ready = S.sem("pj_xT_ready")
        xhi_ready = S.sem("pj_xhi_ready")
        xlo_ready = S.sem("pj_xlo_ready")
        w_loaded = [S.sem(f"pj_w_loaded{i}") for i in range(2)]
        whi_ready = S.sem("pj_whi_ready")
        wlo_ready = S.sem("pj_wlo_ready")
        unit_done = S.sem("pj_unit_done")
        act_evac = S.sem("pj_act_evac")
        sums_ready = S.sem("pj_sums_ready")
        hmean_ready = S.sem("pj_hmean_ready")
        hrstd_ready = S.sem("pj_hrstd_ready")
        scaled = S.sem("pj_scaled")
        dve_evac = S.sem("pj_dve_evac")
        stored = [S.sem(f"pj_stored{i}") for i in range(NO)]

        units, first_tile = [], [0, len(HALVES[0])]
        for hf, tiles in enumerate(HALVES):
            base = tiles[0][0]
            n = sum(r for _, r in tiles)
            for g in range(NG):
                if g in (QC, FC):
                    for e in range(G // P):
                        for c0, cn in blocks_of(n):
                            units.append((hf, g, e, base + c0, cn))
                else:
                    for t0, r in tiles:
                        units.append((hf, g, 0, t0, r))
        NORMED = {QKA: (0, 8, 0), VQ: (WH, 4, 2), KV: (0, 4, 3)}
        BY_DVE = (QKA, VQ, KV, FC, GC)

        first_unit = {}
        for n, u in enumerate(units):
            first_unit.setdefault(u[0] * NG + u[1], n)
        tile_slot = [max(0, i - 1) for i in range(len(HALVES[0]))]
        tile_slot += [first_unit[NG - 1] + i + 1 for i in range(len(HALVES[1]))]
        tiles_at = {}
        for n, slot in enumerate(tile_slot):
            tiles_at.setdefault(slot, []).append(n)
        KH = KD // 2

        def columns(n):
            base = HALVES[n >= first_tile[1]][0][0]
            return slice(TILES[n][0] - base, TILES[n][0] - base + TILES[n][1])

        def units_upto_group(m):
            return sum(1 for u in units if u[0] * NG + u[1] <= m)

        def dve_units(n):
            return sum(1 for u in units[:n + 1] if u[1] in BY_DVE)

        def normed_units(n):
            return sum(1 for u in units[:n + 1] if u[1] in NORMED)

        def wait_whole(eng, n):
            if units[n][1] in BY_DVE:
                eng.wait_ge(dve_evac, dve_units(n))
            else:
                eng.wait_ge(act_evac, n + 1)

        def stores(n):
            hf, g, e, t0, r = units[n]
            if g == QC:
                return [(tr[0, e, :, t0:t0 + r], (slice(0, P), slice(0, r)), 0)]
            if g == FC:
                return [(tr[1, e, :, t0:t0 + r], (slice(0, P), slice(0, r)), 0),
                        (tr[2, e, :, t0:t0 + r], (slice(0, P), slice(0, r)), 1)]
            out = [(proj[g, t0:t0 + r, :], (slice(0, r), slice(0, G)), 0)]
            for name, gg, c in (("ak", QKA, WH), ("av", VQ, 0), ("bk", KV, 0), ("bv", KV, WH)):
                if g != gg:
                    continue
                if t0 == SEQ:
                    dst = outs[name + "s"]
                elif name[0] == "a":
                    dst = outs[name + "p"][t0:t0 + r, :]
                elif t0 >= SEQ - PREV * CHUNK:
                    q = t0 - (SEQ - PREV * CHUNK)
                    dst = outs[name + "p"][q:q + r, :]
                else:
                    continue
                out.append((dst, (slice(0, r), slice(c, c + WH)), 0))
            return out

        def stored_count(n):
            return 16 * sum(len(stores(k)) for k in range(n % NO, n + 1, NO))

        block = ctx.enter_context(nc.Block())

        def load_w(sp, m):
            g = m % NG
            for h in range(2):
                if m >= 1:
                    sp.wait_ge(whi_ready, 2 * m - 1 + h)
                    sp.wait_ge(wlo_ready, 2 * m - 1 + h)
                sp.dma_start(wst[:, h * KH:(h + 1) * KH, :],
                             w_in[h * KH * P:(h + 1) * KH * P, g * G:(g + 1) * G].rearrange("(k p) n -> p k n", p=P)
                             ).then_inc(w_loaded[h], 16)

        @block.sync
        def _(sp):
            def load_x(n):
                (t0, r) = TILES[n]
                if n >= 2:
                    sp.wait_ge(xs_ready, n - 1)
                sp.dma_start(xin[n % 2][0:r, :], x(t0, r)).then_inc(x_loaded[n % 2], 16)

            load_x(0)
            sp.dma_start(grow[:, :], bcast_rows(norm_mix, P)).then_inc(consts, 16)
            load_x(1)
            load_w(sp, 0)
            sp.dma_start(lraw[:, :], lower_bounds.rearrange("(h p) -> p h", p=P), allow_slow_non_contiguous=True
                         ).then_inc(more_consts, 16)
            sp.dma_start(onr[:, :], bcast_rows(onorm, P)).then_inc(more_consts, 16)
            for i, g in enumerate(gains):
                sp.dma_start(gain[:, i, :], bcast_rows(g, P)).then_inc(more_consts, 16)
            for n, (hf, g, e, t0, r) in enumerate(units):
                for j in tiles_at.get(n, []):
                    if j + 2 < len(TILES):
                        load_x(j + 2)
                if n == 0:
                    load_w(sp, 1)
                wait_whole(sp, n)
                for dst, (ps_, cs), which in stores(n):
                    src = (ob, sq)[which][n % NO]
                    sp.dma_start(dst, src[ps_, cs]).then_inc(stored[n % NO], 16)
                m = hf * NG + g
                if n == first_unit[m] and m + 2 < 2 * NG:
                    load_w(sp, m + 2)
            for n in range(len(units) - NO, len(units)):
                sp.wait_ge(stored[n % NO], stored_count(n))

        @block.gpsimd
        def _(pool):
            nc.gpsimd.memset(ident[:, :], 0.0).then_inc(ident_step, 1)
            nc.gpsimd.memset(minus_half[:, :], -0.5).then_inc(ident_step, 1)
            pool.wait_ge(ident_step, 2)
            nc.gpsimd.affine_select(out=ident[:, :], in_=ident[:, :], compare_op=ALU.not_equal, fill=1.0,
                                    base=0, pattern=[[-1, P]], channel_multiplier=1).then_inc(ident_step, 1)
            def inverse_norm(n):
                r = TILES[n][1]
                pool.wait_ge(squared, n + 1)
                nc.gpsimd.tensor_scalar(rstd[0:r, n:n + 1], ss[0:r, n:n + 1], 1.0 / D, EPS,
                                        ALU.mult, ALU.add).then_inc(mean_ready, 1)
                pool.wait_ge(mean_ready, n + 1)
                nc.gpsimd.tensor_tensor(rstd[0:r, n:n + 1], rstd[0:r, n:n + 1], minus_half[0:r, 0:1],
                                        ALU.pow).then_inc(rstd_ready, 1)

            inverse_norm(0)
            for n, (hf, g, e, t0, r) in enumerate(units):
                for j in tiles_at.get(n, []):
                    if j + 1 < len(TILES):
                        inverse_norm(j + 1)
                if g in NORMED:
                    k = normed_units(n)
                    c, nh, _ = NORMED[g]
                    b = n % NO
                    pool.wait_ge(sums_ready, k)
                    nc.gpsimd.tensor_scalar(hr[b][0:r, 0:nh], hs[b][0:r, 0:nh], 1.0 / DH, EPS,
                                            ALU.mult, ALU.add).then_inc(hmean_ready, 1)
                    pool.wait_ge(hmean_ready, k)
                    nc.gpsimd.tensor_tensor(hr[b][0:r, 0:nh], hr[b][0:r, 0:nh],
                                            minus_half[0:r, 0:nh], ALU.pow).then_inc(hrstd_ready, 1)

        @block.scalar
        def _(act):
            def split_w(m):
                for h in range(2):
                    act.wait_ge(w_loaded[h], 16 * (m + 1))
                    if m >= 2:
                        act.wait_ge(unit_done, units_upto_group(m - 2))
                    ks = slice(h * KH, (h + 1) * KH)
                    nc.scalar.activation(whi[m % 2][:, ks, :], wst[:, ks, :], ACT.Copy).then_inc(whi_ready, 1)

            def square(n):
                r = TILES[n][1]
                act.wait_ge(x_loaded[n % 2], 16 * (n // 2 + 1))
                if n >= 2:
                    act.wait_ge(xT_ready, n - 1)
                nc.scalar.activation(xs[n % 2][0:r, :], xin[n % 2][0:r, :], ACT.Square,
                                     accum_out=ss[0:r, n:n + 1]).then_inc(squared, 1)

            square(0)
            for n, (hf, g, e, t0, r) in enumerate(units):
                for j in tiles_at.get(n, []):
                    if j + 1 < len(TILES):
                        square(j + 1)
                    act.wait_ge(xT_ready, j + 1)
                    if j >= first_tile[1]:
                        act.wait_ge(unit_done, min(first_unit[NG - 1] + j - first_tile[1] + 1,
                                                   first_unit[NG]))
                    nc.scalar.activation(xhi[:, :, columns(j)], psT[j % 2][:, :, 0:TILES[j][1]],
                                         ACT.Copy).then_inc(xhi_ready, 1)
                if n == 0:
                    split_w(0)
                    act.wait_ge(lchain, 1)
                    nc.scalar.activation(lexp[:, :], lsm[:, :], ACT.Exp).then_inc(lexp_ready, 1)
                m = hf * NG + g
                if n == first_unit[m] and m + 1 < 2 * NG:
                    split_w(m + 1)
                b = n % NO
                rows, cols = (P, r) if g in (QC, FC) else (r, G)
                act.wait_ge(unit_done, n + 1)
                if n >= NO:
                    act.wait_ge(stored[b], stored_count(n - NO))
                if g in NORMED:
                    last = nc.scalar.activation(sq[b][0:r, :], psO[b][0:r, :], ACT.Square)
                elif g == GC:
                    last = nc.scalar.activation(sq[b][0:r, :], psO[b][0:r, :], ACT.Sigmoid)
                elif g == FC:
                    nc.scalar.activation(ob[b][:, 0:r], psO[b][:, 0:r], ACT.Sigmoid)
                    last = nc.scalar.activation(sq[b][:, 0:r], psO[b][:, 0:r], ACT.Sigmoid, scale=-1.0)
                elif g == QC:
                    last = nc.scalar.activation(ob[b][:, 0:r], psO[b][:, 0:r], ACT.Copy,
                                                scale=float(P) ** -0.5)
                else:
                    last = nc.scalar.activation(ob[b][0:r, :], psO[b][0:r, :], ACT.Copy)
                last.then_inc(act_evac, 1)

        @block.vector
        def _(dve):
            def split_w(m):
                for h in range(2):
                    dve.wait_ge(whi_ready, 2 * m + h + 1)
                    if m >= 2:
                        dve.wait_ge(unit_done, units_upto_group(m - 2))
                    ks = slice(h * KH, (h + 1) * KH)
                    nc.vector.tensor_tensor(wlo[m % 2][:, ks, :], wst[:, ks, :], whi[m % 2][:, ks, :].bitcast(F32),
                                            ALU.subtract).then_inc(wlo_ready, 1)

            def scale(n):
                r = TILES[n][1]
                dve.wait_ge(rstd_ready, n + 1)
                nc.vector.scalar_tensor_tensor(out=xs[n % 2][0:r, :], in0=xin[n % 2][0:r, :],
                                               scalar=rstd[0:r, n:n + 1], in1=grow[0:r, :],
                                               op0=ALU.mult, op1=ALU.mult).then_inc(xs_ready, 1)

            dve.wait_ge(consts, 16)
            scale(0)
            for n, (hf, g, e, t0, r) in enumerate(units):
                for j in tiles_at.get(n, []):
                    if j + 1 < len(TILES):
                        scale(j + 1)
                    dve.wait_ge(xhi_ready, j + 1)
                    nc.vector.tensor_tensor(xlo[:, :, columns(j)], psT[j % 2][:, :, 0:TILES[j][1]],
                                            xhi[:, :, columns(j)].bitcast(F32), ALU.subtract
                                            ).then_inc(xlo_ready, 1)
                if n == 0:
                    split_w(0)
                    dve.wait_ge(more_consts, 16 * 6)
                    nc.vector.tensor_tensor(lsm[:, :], lraw[:, :], lraw[:, :], ALU.subtract).then_inc(lchain, 1)
                    dve.wait_ge(lexp_ready, 1)
                    nc.vector.reciprocal(lb[:, :], lexp[:, :]).then_inc(lchain, 1)
                    dve.wait_ge(lchain, 2)
                    nc.vector.tensor_tensor(lsm[:, :], lexp[:, :], lb[:, :], ALU.mult).then_inc(lchain, 1)
                    dve.wait_ge(lchain, 3)
                    nc.vector.tensor_tensor(lb[:, :], lsm[:, :], lsm[:, :], ALU.subtract).then_inc(lchain, 1)
                    dve.wait_ge(lchain, 4)
                    nc.vector.tensor_scalar(oml[:, :], lb[:, :], -1.0, 1.0, ALU.mult, ALU.add).then_inc(lchain, 1)
                    nc.vector.tensor_scalar(lbf[:, :], lb[:, :], 1e-30, None, ALU.max).then_inc(lchain, 1)
                    dve.wait_ge(lchain, 6)
                m = hf * NG + g
                if n == first_unit[m] and m + 1 < 2 * NG:
                    split_w(m + 1)
                b = n % NO
                if g not in BY_DVE:
                    continue
                dve.wait_ge(act_evac, n + 1)
                if g in NORMED:
                    k = normed_units(n)
                    c, nh, gi = NORMED[g]
                    seg = slice(c, c + nh * DH)
                    nc.vector.tensor_reduce(hs[b][0:r, 0:nh],
                                            sq[b][0:r, seg].rearrange("p (h d) -> p h d", d=DH),
                                            axis=AX.X, op=ALU.add).then_inc(sums_ready, 1)
                    if nh == 4:
                        other = slice(WH - c, 2 * WH - c)
                        nc.vector.tensor_copy(ob[b][0:r, other], psO[b][0:r, other])
                    dve.wait_ge(hrstd_ready, k)
                    o3 = ob[b][0:r, seg].rearrange("p (h d) -> p h d", d=DH)
                    nc.vector.tensor_tensor(o3, psO[b][0:r, seg].rearrange("p (h d) -> p h d", d=DH),
                                            hr[b][0:r, 0:nh].unsqueeze(2).to_broadcast([r, nh, DH]),
                                            ALU.mult).then_inc(scaled, 1)
                    dve.wait_ge(scaled, k)
                    if nh == 8:
                        o4 = ob[b][0:r, :].rearrange("p (a h d) -> p a h d", a=2, d=DH)
                        last = nc.vector.tensor_tensor(
                            o4, o4, gain[0:r, 0:2, :].unsqueeze(2).to_broadcast([r, 2, 4, DH]), ALU.mult)
                    else:
                        last = nc.vector.tensor_tensor(
                            o3, o3, gain[0:r, gi:gi + 1, :].to_broadcast([r, nh, DH]), ALU.mult)
                elif g == FC:
                    nc.vector.tensor_scalar(ob[b][:, 0:r], ob[b][:, 0:r], oml[:, e:e + 1], lbf[:, e:e + 1],
                                            ALU.mult, ALU.add)
                    last = nc.vector.tensor_scalar(sq[b][:, 0:r], sq[b][:, 0:r], oml[:, e:e + 1], None, ALU.mult)
                else:
                    nc.vector.tensor_tensor(ob[b][0:r, :], psO[b][0:r, :], sq[b][0:r, :],
                                            ALU.mult).then_inc(gated, 1)
                    dve.wait_ge(gated, sum(1 for u in units[:n + 1] if u[1] == GC))
                    o3 = ob[b][0:r, :].rearrange("p (h d) -> p h d", h=H)
                    last = nc.vector.tensor_tensor(o3, o3, onr[0:r, :].unsqueeze(1).to_broadcast([r, H, P]), ALU.mult)
                last.then_inc(dve_evac, 1)

        @block.tensor
        def _(pe):
            pe.wait_ge(ident_step, 3)
            for n, (hf, g, e, t0, r) in enumerate(units):
                for j in tiles_at.get(n, []):
                    pe.wait_ge(xs_ready, j + 1)
                    if j >= 2:
                        pe.wait_ge(xlo_ready, j - 1)
                    rj = TILES[j][1]
                    for k in range(KD):
                        last = nc.tensor.transpose(psT[j % 2][:, k, 0:rj], xs[j % 2][0:rj, k * P:(k + 1) * P],
                                                   ident[0:rj, 0:rj])
                    last.then_inc(xT_ready, 1)
                base, m = HALVES[hf][0][0], hf * NG + g
                pe.wait_ge(xlo_ready, first_tile[hf] + (n - first_unit[m] + 1 if g == 0 else len(HALVES[hf])))
                if n >= NO:
                    wait_whole(pe, n - NO)
                c = slice(t0 - base, t0 - base + r)
                passes = [(xhi, whi), (xhi, wlo), (xlo, whi)]
                for k in range(KD):
                    if n == first_unit[m] and k % KH == 0:
                        pe.wait_ge(wlo_ready, 2 * m + k // KH + 1)
                    for j, (xa, wa) in enumerate(passes):
                        st, sp_ = k == 0 and j == 0, k == KD - 1 and j == 2
                        wt = wa[m % 2]
                        if g in (QC, FC):
                            last = nc.tensor.matmul(psO[n % NO][:, 0:r], wt[:, k, e * P:(e + 1) * P],
                                                    xa[:, k, c], start=st, stop=sp_)
                        else:
                            last = nc.tensor.matmul(psO[n % NO][0:r, :], xa[:, k, c], wt[:, k, :],
                                                    start=st, stop=sp_)
                last.then_inc(unit_done, 1)


def attend(nc, kind, q_src, k_src, v_src, bias, mix):
    A = kind == "A"
    SMP = PAST + NEW
    NC = PAST // P
    steps = [("s", j * P, P, False) for j in range(NC)] + [("s", PAST, NEW, True)]
    steps += [("p", j * P, P, True) for j in range(NT)]
    NSTEP = len(steps)
    kt0 = {"s": 0, "p": SMP}
    vt0 = {"s": 0, "p": NC + 1}
    units = []
    for s, (seq, t0, r, att) in enumerate(steps):
        if not att:
            continue
        for h in range(H):
            end = t0 + r
            if A:
                c = (end - 1) // 512
                while c >= 0:
                    c1 = min(end, 512 * (c + 1))
                    units.append((s, h, 512 * c, c1 - 512 * c, c1 == end, c == 0))
                    c -= 1
            else:
                k0 = max(0, t0 - PREV * CHUNK)
                units.append((s, h, k0, end - k0, True, True))
    NU = len(units)
    rows_of = [units[n][:2] for n in range(NU)]
    row_ids = sorted(set(rows_of))
    row_no = {x: i for i, x in enumerate(row_ids)}
    row_last = {row_no[rows_of[n]]: n for n in range(NU)}
    att_steps = [s for s in range(NSTEP) if steps[s][3]]
    att_no = {s: i for i, s in enumerate(att_steps)}
    step_last = {s: max(n for n in range(NU) if units[n][0] == s) for s in att_steps}
    step_first = {s: min(n for n in range(NU) if units[n][0] == s) for s in att_steps}
    if A:
        L_U, L_SCAN, L_W, L_T, L_TOUT, L_AV = 1, 2, 3, 4, 5, 6
    else:
        L_U, L_W, L_T, L_TOUT, L_AV = 1, 2, 3, 4, 5
    L_O = L_AV + 1
    ctx = ExitStack()
    with ctx:
        S = Space(nc, ctx)
        pre = "at" + kind
        ZB = 4 if A else 2
        ZW = 512 if A else 1024
        WB = 2 if A else 1
        WW = 4 if A else 5
        NW = 3
        ident = S.sb(pre + "ident", [P, P])
        kn = [S.sb(pre + f"kn{i}", [P, H, DH]) for i in range(2)]
        qn = [S.sb(pre + f"qn{i}", [P, H, 2, DH]) for i in range(2)]
        khl = [S.sb(pre + f"khl{i}", [P, H, 2, DH]) for i in range(2)]
        KT = S.sb(pre + "KT", [P, H, SMP + SEQ], F32R)
        V = S.sb(pre + "V", [P, NC + 1 + NT, WH])
        qhi = [S.sb(pre + f"qhi{i}", [P, H, P], F32R) for i in range(2)]
        qlo = [S.sb(pre + f"qlo{i}", [P, H, P], F32R) for i in range(2)]
        ub = [S.sb(pre + f"ub{i}", [P, 512 if A else BW]) for i in range(NW)]
        wb = [S.sb(pre + f"wb{i}", [P, 512 if A else BW]) for i in range(NW)]
        wT = [S.sb(pre + f"wT{i}", [P, WW, P]) for i in range(2)]
        o = [S.sb(pre + f"o{i}", [P, WH]) for i in range(2)]
        if A:
            cp = [S.sb(pre + f"cp{i}", [P, SEQ + 1]) for i in range(2)]
        else:
            bt = S.sb(pre + "bt", [P, H, BW])
            btr = S.sb(pre + "btr", [P, H, BW])
            flip = S.sb(pre + "flip", [P, P])
            tb = S.sb(pre + "tb", [H, 2 * CLIP + 1])
            ln = S.sb(pre + "ln", [H, NLINE])
            mx = [S.sb(pre + f"mx{i}", [P, 1]) for i in range(NW)]
            nmx = [S.sb(pre + f"nmx{i}", [P, 1]) for i in range(NW)]
            den = [S.sb(pre + f"den{i}", [P, H]) for i in range(2)]
            rden = S.sb(pre + "rden", [P, H])
        psZ = [S.ps(pre + f"psZ{i}", [P, ZW]) for i in range(ZB)]
        psT = S.ps(pre + "psT", [P, H, P])
        psW = [S.ps(pre + f"psW{i}", [P, 4 if A else 8, P]) for i in range(WB)]
        psO = S.ps(pre + "psO", [P, WH])

        init = S.sem(pre + "init")
        loaded = [S.sem(pre + f"loaded{i}") for i in range(2)]
        bias_loaded = S.sem(pre + "bias_loaded")
        table_loaded = S.sem(pre + "table_loaded")
        line_ready = S.sem(pre + "line_ready")
        turned = S.sem(pre + "turned")
        bt_ready = S.sem(pre + "bt_ready")
        line_stored = S.sem(pre + "line_stored")
        khi_ready = S.sem(pre + "khi_ready")
        khl_ready = S.sem(pre + "khl_ready")
        kT_ready = S.sem(pre + "kT_ready")
        kT_out = S.sem(pre + "kT_out")
        qT_ready = S.sem(pre + "qT_ready")
        qhi_ready = S.sem(pre + "qhi_ready")
        qlo_ready = S.sem(pre + "qlo_ready")
        z_ready = S.sem(pre + "z_ready")
        u_ready = S.sem(pre + "u_ready")
        masked = S.sem(pre + "masked")
        scanned = S.sem(pre + "scanned")
        w_ready = S.sem(pre + "w_ready")
        wT_ready = S.sem(pre + "wT_ready")
        wT_out = S.sem(pre + "wT_out")
        av_done = S.sem(pre + "av_done")
        o_ready = S.sem(pre + "o_ready")
        max_ready = S.sem(pre + "max_ready")
        bias_added = S.sem(pre + "bias_added")
        nmax_ready = S.sem(pre + "nmax_ready")
        rden_ready = S.sem(pre + "rden_ready")
        stored = [S.sem(pre + f"stored{i}") for i in range(2)]

        def loads_upto(s):
            return 16 * sum(4 if steps[k][3] else 2 for k in range(s % 2, s + 1, 2))

        def att_upto(s):
            return sum(1 for k in att_steps if k <= s)

        def masks_upto(n):
            return sum(1 for u in units[:n + 1] if u[4])

        FIRST = -4 * (NC + 1)
        prep_at = {sidx: FIRST + 4 * sidx if sidx <= NC else step_first[sidx - 1] for sidx in range(NSTEP)}
        prep_step = {t: sidx for sidx, t in prep_at.items()}
        TURNS = range(FIRST - 4, NU + L_O + 1)

        def outputs_due(i):
            return [sidx for sidx in att_steps if step_last[sidx] + L_O == i]

        block = ctx.enter_context(nc.Block())

        @block.sync
        def _(sp):
            if not A:
                table, line = bias
                sp.dma_start(tb[:, :], table).then_inc(table_loaded, 16)
            for turn in TURNS:
                if turn == FIRST and not A:
                    sp.wait_ge(line_ready, 1)
                    sp.dma_start(line, ln[:, :]).then_inc(line_stored, 16)
                    sp.wait_ge(line_stored, 16)
                    for h in range(H):
                        rows = bass.AP(line.tensor, line.offset + h * NLINE, [[1, P], [1, BW]])
                        sp.dma_start(btr[:, h, :], rows).then_inc(bias_loaded, 16)
                i = prep_step.get(turn + 4)
                if i is not None:
                    seq, t0, r, att = steps[i]
                    if i >= 2:
                        sp.wait_ge(khl_ready, i - 1)
                        if att_upto(i - 2):
                            sp.wait_ge(qT_ready, att_upto(i - 2))
                    sp.dma_start(kn[i % 2][0:r, :, :], k_src(seq, t0, r)).then_inc(loaded[i % 2], 16)
                    sp.dma_start(V[0:r, vt0[seq] + t0 // P, :], v_src(seq, t0, r)).then_inc(loaded[i % 2], 16)
                    if att:
                        for copy in range(2):
                            sp.dma_start(qn[i % 2][0:r, :, copy, :], q_src(seq, t0, r)).then_inc(loaded[i % 2], 16)
                for step in outputs_due(turn):
                    seq, t0, r, _ = steps[step]
                    n = att_no[step]
                    sp.wait_ge(o_ready, n + 1)
                    row = t0 if seq == "p" else SEQ
                    sp.dma_start(mix[row:row + r, :], o[n % 2][0:r, :]).then_inc(stored[n % 2], 16)
            for i in range(2):
                sp.wait_ge(stored[i], 16 * len(range(i, len(att_steps), 2)))

        @block.gpsimd
        def _(pool):
            nc.gpsimd.memset(ident[:, :], 0.0).then_inc(init, 1)
            if A:
                for i in range(2):
                    nc.gpsimd.memset(cp[i][:, SEQ:SEQ + 1], 1.0).then_inc(init, 1)
                pool.wait_ge(init, 3)
            else:
                pool.wait_ge(init, 1)
            nc.gpsimd.affine_select(out=ident[:, :], in_=ident[:, :], compare_op=ALU.not_equal, fill=1.0,
                                    base=0, pattern=[[-1, P]], channel_multiplier=1).then_inc(init, 1)
            if not A:
                nc.gpsimd.memset(flip[:, :], 0.0).then_inc(init, 1)
                pool.wait_ge(init, 3)
                nc.gpsimd.affine_select(out=flip[:, :], in_=flip[:, :], compare_op=ALU.not_equal, fill=1.0,
                                        base=1 - P, pattern=[[1, P]], channel_multiplier=1).then_inc(init, 1)
                pool.wait_ge(init, 4)
                pool.wait_ge(bt_ready, H)
                nc.gpsimd.memset(bt[0:CHUNK, :, BW - CHUNK:BW], NEG).then_inc(init, 1)
                pool.wait_ge(init, 5)
                nc.gpsimd.memset(bt[CHUNK:P, :, 0:CHUNK], NEG).then_inc(init, 1)
                return
            for turn in TURNS:
                i = turn - L_U
                if 0 <= i < NU and units[i][4]:
                    s, h, k0, kn_, _, _ = units[i]
                    r = steps[s][2]
                    d = ub[i % NW][0:r, kn_ - r:kn_]
                    pool.wait_ge(u_ready, i + 1)
                    nc.gpsimd.affine_select(out=d, in_=d, compare_op=ALU.is_gt, fill=1.0, base=0,
                                            pattern=[[-1, r]], channel_multiplier=1).then_inc(masked, 1)

        @block.scalar
        def _(act):
            for turn in TURNS:
                j = turn - L_TOUT
                if 0 <= j < NU:
                    s, h, k0, w, _, _ = units[j]
                    r = steps[s][2]
                    act.wait_ge(wT_ready, j + 1)
                    if j >= 2:
                        act.wait_ge(av_done, j - 1)
                    full = w // P
                    last = None
                    if full:
                        last = nc.scalar.activation(wT[j % 2][:, 0:full, 0:r], psW[j % WB][:, 0:full, 0:r], ACT.Copy)
                    if w % P:
                        last = nc.scalar.activation(wT[j % 2][0:w % P, full, 0:r],
                                                    psW[j % WB][0:w % P, full, 0:r], ACT.Copy)
                    last.then_inc(wT_out, 1)
                i = turn - (L_U if A else L_W)
                if 0 <= i < NU:
                    s, h, k0, w, _, _ = units[i]
                    r = steps[s][2]
                    if A:
                        act.wait_ge(z_ready, i + 1)
                        if i >= NW:
                            act.wait_ge(scanned, i - NW + 1)
                        nc.scalar.activation(ub[i % NW][0:r, 0:w], psZ[i % ZB][0:r, 0:w], ACT.Sigmoid,
                                             scale=-float(DH) ** -0.5).then_inc(u_ready, 1)
                    else:
                        act.wait_ge(nmax_ready, i + 1)
                        if i >= NW:
                            act.wait_ge(wT_ready, i - NW + 1)
                        d = den[att_no[s] % 2]
                        if h == 0 and att_no[s] >= 2:
                            act.wait_ge(rden_ready, att_no[s] - 1)
                        nc.scalar.activation(wb[i % NW][0:r, 0:w], ub[i % NW][0:r, 0:w], ACT.Exp,
                                             bias=nmx[i % NW][0:r, :], accum_out=d[0:r, h:h + 1]
                                             ).then_inc(w_ready, 1)
                i = prep_step.get(turn)
                if i is not None:
                    seq, t0, r, att = steps[i]
                    c = kt0[seq] + t0
                    act.wait_ge(kT_ready, i + 1)
                    nc.scalar.activation(KT[:, :, c:c + r], psT[:, :, 0:r], ACT.Copy).then_inc(kT_out, 1)
                i = prep_step.get(turn - 1)
                if i is not None and steps[i][3]:
                    r = steps[i][2]
                    act.wait_ge(qT_ready, att_upto(i))
                    if att_no[i] >= 2:
                        act.wait_ge(z_ready, step_last[att_steps[att_no[i] - 2]] + 1)
                    b = att_no[i] % 2
                    nc.scalar.activation(qhi[b][:, :, 0:r], psT[:, :, 0:r], ACT.Copy).then_inc(qhi_ready, 1)

        @block.vector
        def _(dve):
            if not A:
                dve.wait_ge(table_loaded, 16)
                far = NLINE - 2 * CLIP
                nc.vector.tensor_copy(ln[:, 0:far], tb[:, 2 * CLIP:2 * CLIP + 1].to_broadcast([H, far]))
                nc.vector.tensor_copy(ln[:, far:NLINE], tb[:, 1:2 * CLIP + 1][:, ::-1]).then_inc(line_ready, 1)
            for turn in TURNS:
                if turn == -1 and not A:
                    for h in range(H):
                        dve.wait_ge(turned, h + 1)
                        nc.vector.tensor_copy(bt[:, h, :], psZ[h % 2][:, 0:BW]).then_inc(bt_ready, 1)
                i = prep_step.get(turn + 1)
                if i is not None:
                    seq, t0, r, att = steps[i]
                    b = i % 2
                    dve.wait_ge(loaded[b], loads_upto(i))
                    if i >= 2:
                        dve.wait_ge(kT_ready, i - 1)
                    nc.vector.tensor_copy(khl[b][0:r, :, 0, :].bitcast(F32R), kn[b][0:r, :, :]).then_inc(khi_ready, 1)
                    dve.wait_ge(khi_ready, i + 1)
                    nc.vector.tensor_tensor(khl[b][0:r, :, 1, :], kn[b][0:r, :, :], khl[b][0:r, :, 0, :],
                                            ALU.subtract).then_inc(khl_ready, 1)
                i = prep_step.get(turn - 2)
                if i is not None and steps[i][3]:
                    r = steps[i][2]
                    dve.wait_ge(qhi_ready, att_upto(i))
                    q = att_no[i] % 2
                    nc.vector.tensor_tensor(qlo[q][:, :, 0:r], psT[:, :, 0:r],
                                            qhi[q][:, :, 0:r].bitcast(F32), ALU.subtract).then_inc(qlo_ready, 1)
                i = turn - (L_SCAN if A else L_U)
                if 0 <= i < NU:
                    s, h, k0, w, last_chunk, _ = units[i]
                    r, end = steps[s][2], steps[s][1] + steps[s][2]
                    u = ub[i % NW]
                    if A:
                        a = SEQ - end + k0
                        row = row_no[(s, h)]
                        c = cp[row % 2]
                        dve.wait_ge(u_ready, i + 1)
                        if last_chunk:
                            dve.wait_ge(masked, masks_upto(i))
                            if row >= 2:
                                dve.wait_ge(w_ready, row_last[row - 2] + 1)
                            init_v = 1.0
                        else:
                            dve.wait_ge(scanned, i)
                            init_v = c[0:r, a + w:a + w + 1]
                        nc.vector.tensor_tensor_scan(out=c[0:r, a:a + w][:, ::-1], data0=u[0:r, 0:w][:, ::-1],
                                                     data1=u[0:r, 0:w][:, ::-1], initial=init_v,
                                                     op0=ALU.mult, op1=ALU.bypass).then_inc(scanned, 1)
                    else:
                        dve.wait_ge(z_ready, i + 1)
                        if i == 0:
                            dve.wait_ge(init, 6)
                        if i >= NW:
                            dve.wait_ge(w_ready, i - NW + 1)
                        b0 = BW - w if steps[s][0] == "p" else 0
                        nc.vector.scalar_tensor_tensor(out=u[0:r, 0:w], in0=psZ[i % ZB][0:r, 0:w],
                                                       scalar=float(DH) ** -0.5, in1=bt[0:r, h, b0:b0 + w],
                                                       op0=ALU.mult, op1=ALU.add).then_inc(bias_added, 1)
                        dve.wait_ge(bias_added, i + 1)
                        nc.vector.tensor_reduce(mx[i % NW][0:r, :], u[0:r, 0:w], axis=AX.X,
                                                op=ALU.max).then_inc(max_ready, 1)
                        dve.wait_ge(max_ready, i + 1)
                        nc.vector.tensor_scalar(nmx[i % NW][0:r, :], mx[i % NW][0:r, :], -1.0, None,
                                                ALU.mult).then_inc(nmax_ready, 1)
                j = turn - L_W
                if A and 0 <= j < NU:
                    s, h, k0, w, _, _ = units[j]
                    r, end = steps[s][2], steps[s][1] + steps[s][2]
                    a = SEQ - end + k0
                    c = cp[row_no[(s, h)] % 2]
                    dve.wait_ge(scanned, j + 1)
                    if j >= NW:
                        dve.wait_ge(wT_ready, j - NW + 1)
                    nc.vector.tensor_tensor(wb[j % NW][0:r, 0:w], c[0:r, a + 1:a + 1 + w], c[0:r, a:a + w],
                                            ALU.subtract).then_inc(w_ready, 1)
                for s in outputs_due(turn):
                    out_no = att_no[s]
                    r = steps[s][2]
                    dve.wait_ge(av_done, step_last[s] + 1)
                    if out_no >= 2:
                        dve.wait_ge(stored[out_no % 2], 16 * (out_no // 2))
                    ob = o[out_no % 2]
                    if A:
                        nc.vector.tensor_copy(ob[0:r, :], psO[0:r, :]).then_inc(o_ready, 1)
                    else:
                        nc.vector.reciprocal(rden[0:r, :], den[out_no % 2][0:r, :]).then_inc(rden_ready, 1)
                        dve.wait_ge(rden_ready, out_no + 1)
                        nc.vector.tensor_tensor(ob[0:r, :].rearrange("p (h d) -> p h d", h=H),
                                                psO[0:r, :].rearrange("p (h d) -> p h d", h=H),
                                                rden[0:r, :].unsqueeze(2).to_broadcast([r, H, DH]),
                                                ALU.mult).then_inc(o_ready, 1)

        @block.tensor
        def _(pe):
            pe.wait_ge(init, 4)
            for turn in TURNS:
                if turn == -2 and not A:
                    pe.wait_ge(bias_loaded, 16 * H)
                    for h in range(H):
                        if h >= 2:
                            pe.wait_ge(bt_ready, h - 1)
                        for x0 in range(0, BW, 512):
                            x1 = min(BW, x0 + 512)
                            last = nc.tensor.matmul(psZ[h % 2][:, x0:x1], flip[:, :], btr[:, h, x0:x1],
                                                    start=True, stop=True)
                        last.then_inc(turned, 1)
                i = prep_step.get(turn)
                if i is not None:
                    seq, t0, r, att = steps[i]
                    pe.wait_ge(khl_ready, i + 1)
                    if att_upto(i - 1):
                        pe.wait_ge(qlo_ready, att_upto(i - 1))
                    if i >= 1:
                        pe.wait_ge(kT_out, i)
                    for h in range(H):
                        last = nc.tensor.transpose(psT[:, h, 0:r], khl[i % 2][0:r, h, :, :], ident[0:r, 0:r])
                    last.then_inc(kT_ready, 1)
                i = prep_step.get(turn - 1)
                if i is not None and steps[i][3]:
                    r = steps[i][2]
                    pe.wait_ge(kT_out, i + 1)
                    for h in range(H):
                        last = nc.tensor.transpose(psT[:, h, 0:r], qn[i % 2][0:r, h, :, :], ident[0:r, 0:r])
                    last.then_inc(qT_ready, 1)
                i = turn
                if 0 <= i < NU:
                    s, h, k0, w, _, _ = units[i]
                    seq, t0, r, _ = steps[s]
                    q = att_no[s] % 2
                    if i == step_first[s]:
                        pe.wait_ge(qlo_ready, att_upto(s))
                    if i == 0 and not A:
                        pe.wait_ge(bt_ready, H)
                    if i >= ZB:
                        if A:
                            pe.wait_ge(u_ready, i - ZB + 1)
                        else:
                            pe.wait_ge(bias_added, i - ZB + 1)
                    c0 = kt0[seq] + k0
                    for x0 in range(0, w, 512):
                        x1 = min(w, x0 + 512)
                        for qq, first in ((qhi, True), (qlo, False)):
                            last = nc.tensor.matmul(psZ[i % ZB][0:r, x0:x1], qq[q][:, h, 0:r],
                                                    KT[:, h, c0 + x0:c0 + x1], start=first, stop=not first)
                    last.then_inc(z_ready, 1)
                j = i - L_AV
                if 0 <= j < NU:
                    s, h, k0, w, first, last_ = units[j]
                    seq, t0, r, _ = steps[s]
                    pe.wait_ge(wT_out, j + 1)
                    if j == step_first[s] and att_no[s] >= 1:
                        pe.wait_ge(o_ready, att_no[s])
                    nb = -(-w // P)
                    for b in range(nb):
                        kr = min(P, w - b * P)
                        last = nc.tensor.matmul(psO[0:r, h * DH:(h + 1) * DH], wT[j % 2][0:kr, b, 0:r],
                                                V[0:kr, vt0[seq] + k0 // P + b, h * DH:(h + 1) * DH],
                                                start=first and b == 0, stop=last_ and b == nb - 1)
                    last.then_inc(av_done, 1)
                j = i - L_T
                if 0 <= j < NU:
                    s, h, k0, w, _, _ = units[j]
                    r = steps[s][2]
                    pe.wait_ge(w_ready, j + 1)
                    if j >= WB:
                        pe.wait_ge(wT_out, j - WB + 1)
                    for b in range(-(-w // P)):
                        kr = min(P, w - b * P)
                        last = nc.tensor.transpose(psW[j % WB][0:kr, b, 0:r], wb[j % NW][0:r, b * P:b * P + kr],
                                                   ident[0:r, 0:r])
                    last.then_inc(wT_ready, 1)


def recur(nc, tr, v_src, g_src, state_in, state_outs, mix):
    tiles = [(SEQ, NEW, True)] + [(t * P, P, t > 0) for t in range(NT)]
    N = len(tiles)
    THR = 2.0 ** -50
    ctx = ExitStack()
    with ctx:
        S = Space(nc, ctx)
        W = H * P
        ident = S.sb("rc_ident", [P, P])
        masks = S.sb("rc_masks", [P, 8, P])
        keep = {r: S.sb(f"rc_keep{r}", [P, H * r]) for r in (P, NEW)}
        minus_half = S.sb("rc_mhalf", [P, H])

        def pair(name, w=W):
            return [S.sb(f"rc_{name}{i}", [P, w]) for i in range(2)]

        NL = 4
        q, f, k, v, g = ([S.sb(f"rc_{z}{i}", [P, W]) for i in range(NL)] for z in ("q", "f", "k", "v", "g"))
        a, b, la, lf, gs, e1, d2, e2, qh, kh = (
            pair(z) for z in ("a", "b", "la", "lf", "gs", "e1", "d2", "e2", "qh", "kh"))
        khn, sqo, on = (pair(z) for z in ("khn", "sqo", "on"))
        so, rs = pair("so", H), pair("rs", H)
        NX = 3
        d, e, x = ([S.sb(f"rc_{z}{i}", [P, W]) for i in range(NX)] for z in ("d", "e", "x"))
        At = {n: S.sb(f"rc_At{n}", [P, H, P]) for n in range(3)}
        St = [S.sb(f"rc_S{i}", [P, H, P]) for i in range(3)]
        NA = 4
        psA = [S.ps(f"rc_psA{i}", [P, H, P]) for i in range(NA)]
        psK = S.ps("rc_psK", [P, H, P])
        psO = [S.ps(f"rc_psO{i}", [P, H, P]) for i in range(2)]
        psS = S.ps("rc_psS", [P, H, P])
        names = """init maskstep ab_ready ln_ready
            lf_ready g_ready d_ready e_ready x_ready a_ready a_out d2_ready e12_ready qk_ready khT_ready khn_ready
            o_done s_done s_out sq_ready so_ready rsm_ready rs_ready osc_ready on_ready state_loaded""".split()
        s = {z: S.sem("rc_" + z) for z in names}
        loaded = [S.sem(f"rc_loaded{i}") for i in range(NL)]
        stored = [S.sem(f"rc_stored{i}") for i in range(2)]
        state_stored = S.sem("rc_state_stored")

        def levels(n):
            r, out = tiles[n][1], []
            m = r // 2
            while m:
                out.append(m)
                m //= 2
            return out

        lev0 = [sum(len(levels(j)) for j in range(n)) for n in range(N + 1)]
        prod0 = [lev0[n] + n for n in range(N + 1)]

        NPOS = 8
        EXP, MULT, PROD, TAKE = 1, 2, 3, 4
        FRONT_A, LN, FRONT_B, FRONT_C, D2, E12 = 1, 3, 4, 5, 3, 8
        QK, KHT, KHN, SPROD, SOUT, OPROD, SQ, RMS, RS, OSC, GATE = 9, 10, 11, 12, 13, 13, 14, 15, 17, 18, 19
        SPOTS = range((N - 1) * NPOS + GATE + 1)

        def tile_at(spot, step):
            n, i = divmod(spot - step, NPOS)
            return n if i == 0 and 0 <= n < N else None

        def level_at(spot, step):
            n, i = divmod(spot - step, NPOS)
            return (n, i) if spot >= step and n < N and i < len(levels(n)) else None

        def product_at(spot, step):
            n, i = divmod(spot - step, NPOS)
            return (n, i) if spot >= step and n < N and i <= len(levels(n)) else None

        def wait_loaded(eng, n):
            eng.wait_ge(loaded[n % NL], 16 * 5 * (n // NL + 1))

        def at(n):
            return At[2] if n == 0 else At[n % 2]

        def flat(buf, n):
            return buf[:, 0:H * tiles[n][1]]

        def heads(buf, n):
            return flat(buf, n).rearrange("p (h t) -> p h t", h=H)

        def blk(buf, n, m):
            return flat(buf, n).rearrange("p (b t) -> p b t", t=2 * m)

        block = ctx.enter_context(nc.Block())

        @block.sync
        def _(sp):
            sp.dma_start(St[0][:, :, :], state_in.rearrange("h k v -> k h v")).then_inc(s["state_loaded"], 16)
            for n in range(N + NL):
                if n < N:
                    t0, r, _ = tiles[n]
                    if n >= NL:
                        sp.wait_ge(s["o_done"], n - NL + 1)
                        sp.wait_ge(s["s_done"], n - NL + 1)
                        sp.wait_ge(s["on_ready"], n - NL + 1)
                    for i, buf in enumerate((q, f, k)):
                        sp.dma_start(heads(buf[n % NL], n), tr[i, :, :, t0:t0 + r].rearrange("h p t -> p h t")
                                     ).then_inc(loaded[n % NL], 16)
                    sp.dma_start(v[n % NL][0:r, :], v_src(t0, r)).then_inc(loaded[n % NL], 16)
                    sp.dma_start(g[n % NL][0:r, :], g_src(t0, r)).then_inc(loaded[n % NL], 16)
                j = n - NL
                if j >= 0:
                    t0, r, _ = tiles[j]
                    sp.wait_ge(s["on_ready"], j + 1)
                    sp.dma_start(mix[t0:t0 + r, :], on[j % 2][0:r, :]).then_inc(stored[j % 2], 16)
                    if j in (0, N - 1):
                        sp.wait_ge(s["s_out"], j + 1)
                        sp.dma_start(state_outs[0 if j else 1].rearrange("h k v -> k h v"),
                                     St[(j + 1) % 3][:, :, :]).then_inc(state_stored, 16)
            for i in range(2):
                sp.wait_ge(stored[i], 16 * len(range(i, N, 2)))
            sp.wait_ge(state_stored, 32)

        @block.gpsimd
        def _(pool):
            nc.gpsimd.memset(ident[:, :], 0.0)
            nc.gpsimd.memset(masks[:, :, :], 0.0)
            nc.gpsimd.memset(minus_half[:, :], -0.5)
            for i in range(3):
                nc.gpsimd.memset(At[i][:, :, :], 0.0)
            for r in (P, NEW):
                last = nc.gpsimd.memset(keep[r][:, :], 1.0)
            last.then_inc(s["maskstep"], 1)
            step = 1
            pool.wait_ge(s["maskstep"], step)
            for r in (P, NEW):
                nc.gpsimd.memset(keep[r][:, :].rearrange("p (h t) -> p h t", h=H)[:, :, 0:1], 0.0)
            for lv in range(7):
                m = 1 << lv
                nc.gpsimd.memset(masks[:, lv, :].rearrange("p (b t) -> p b t", t=2 * m)[:, :, m:2 * m], 1.0)
            nc.gpsimd.affine_select(out=masks[:, 7, :], in_=masks[:, 7, :], compare_op=ALU.not_equal, fill=1.0,
                                    base=0, pattern=[[-1, P]], channel_multiplier=1)
            nc.gpsimd.affine_select(out=ident[:, :], in_=ident[:, :], compare_op=ALU.not_equal, fill=1.0,
                                    base=0, pattern=[[-1, P]], channel_multiplier=1).then_inc(s["maskstep"], 1)
            step += 1
            for lv in range(7):
                m = 1 << lv
                mv = masks[:, lv, :].rearrange("p (b t) -> p b t", t=2 * m)
                for mult, base in ((1, 0), (-1, m - 1)):
                    pool.wait_ge(s["maskstep"], step)
                    nc.gpsimd.affine_select(out=mv, in_=mv, compare_op=ALU.is_ge, fill=0.0, base=base,
                                            pattern=[[-2 * m * mult, P // (2 * m)], [0, 2 * m]],
                                            channel_multiplier=mult).then_inc(s["maskstep"], 1)
                    step += 1
            pool.wait_ge(s["maskstep"], step)
            nc.gpsimd.memset(keep[P][0:1, 0:1], 0.0).then_inc(s["init"], 1)
            for spot in SPOTS:
                if level_at(spot, MULT):
                    n, i = level_at(spot, MULT)
                    m, u = levels(n)[i], lev0[n] + i
                    if i == 0:
                        wait_loaded(pool, n)
                    pool.wait_ge(s["e_ready"], u + 1)
                    if u >= NX:
                        pn = max(j for j in range(N) if lev0[j] <= u - NX)
                        pool.wait_ge(s["a_ready"], prod0[pn] + (u - NX - lev0[pn]) + 1)
                    xv, ev = blk(x[u % NX], n, m), blk(e[u % NX], n, m)
                    nc.gpsimd.tensor_tensor(xv[:, :, 0:m], ev[:, :, 0:m], blk(k[n % NL], n, m)[:, :, 0:m], ALU.mult)
                    nc.gpsimd.tensor_tensor(xv[:, :, m:2 * m], ev[:, :, m:2 * m],
                                            blk(q[n % NL], n, m)[:, :, m:2 * m], ALU.mult).then_inc(s["x_ready"], 1)
                n = tile_at(spot, RS)
                if n is not None:
                    pb, r = n % 2, tiles[n][1]
                    pool.wait_ge(s["so_ready"], n + 1)
                    nc.gpsimd.tensor_scalar(rs[pb][0:r, :], so[pb][0:r, :], 1.0 / P, EPS, ALU.mult,
                                            ALU.add).then_inc(s["rsm_ready"], 1)
                    pool.wait_ge(s["rsm_ready"], n + 1)
                    nc.gpsimd.tensor_tensor(rs[pb][0:r, :], rs[pb][0:r, :], minus_half[0:r, :],
                                            ALU.pow).then_inc(s["rs_ready"], 1)
                n = tile_at(spot, QK)
                if n is not None:
                    bb = n % 2
                    pool.wait_ge(s["e12_ready"], n + 1)
                    if n >= 2:
                        pool.wait_ge(s["o_done"], n - 1)
                        pool.wait_ge(s["khT_ready"], n - 1)
                    nc.gpsimd.tensor_tensor(flat(kh[bb], n), flat(k[n % NL], n), flat(e2[bb], n), ALU.mult)
                    nc.gpsimd.tensor_tensor(flat(qh[bb], n), flat(q[n % NL], n), flat(e1[bb], n),
                                            ALU.mult).then_inc(s["qk_ready"], 1)

        @block.scalar
        def _(act):
            def front(n):
                bb = n % 2
                act.wait_ge(s["ab_ready"], n + 1)
                nc.scalar.activation(flat(la[bb], n), flat(a[bb], n), ACT.Ln)
                nc.scalar.activation(flat(lf[bb], n), flat(b[bb], n), ACT.Ln).then_inc(s["ln_ready"], 1)

            front(0)
            for spot in SPOTS:
                if level_at(spot, EXP):
                    n, i = level_at(spot, EXP)
                    u = lev0[n] + i
                    act.wait_ge(s["d_ready"], u + 1)
                    if u >= NX:
                        act.wait_ge(s["x_ready"], u - NX + 1)
                    nc.scalar.activation(flat(e[u % NX], n), flat(d[u % NX], n), ACT.Exp).then_inc(s["e_ready"], 1)
                n = tile_at(spot, LN)
                if n is not None and n + 1 < N:
                    front(n + 1)
                n = tile_at(spot, KHN)
                if n is not None:
                    r, bb = tiles[n][1], n % 2
                    act.wait_ge(s["khT_ready"], n + 1)
                    if n >= 2:
                        act.wait_ge(s["s_done"], n - 1)
                    nc.scalar.activation(khn[bb][0:r, :].rearrange("p (h t) -> p h t", h=H), psK[0:r, :, :],
                                         ACT.Copy).then_inc(s["khn_ready"], 1)
                n = tile_at(spot, SQ)
                if n is not None:
                    r, bb = tiles[n][1], n % 2
                    act.wait_ge(s["o_done"], n + 1)
                    nc.scalar.activation(sqo[bb][0:r, :].rearrange("p (h t) -> p h t", h=H), psO[bb][0:r, :, :],
                                         ACT.Square).then_inc(s["sq_ready"], 1)
                n = tile_at(spot, E12)
                if n is not None:
                    bb = n % 2
                    act.wait_ge(s["d2_ready"], n + 1)
                    if n >= 2:
                        act.wait_ge(s["s_out"], n - 1)
                    nc.scalar.activation(flat(e1[bb], n), flat(gs[bb], n), ACT.Exp)
                    nc.scalar.activation(flat(e2[bb], n), flat(d2[bb], n), ACT.Exp).then_inc(s["e12_ready"], 1)

        @block.vector
        def _(dve):
            dve.wait_ge(s["init"], 1)

            def front_a(n):
                bb = n % 2
                wait_loaded(dve, n)
                nc.vector.tensor_scalar(flat(a[bb], n), flat(f[n % NL], n), THR, None, ALU.max)
                nc.vector.tensor_scalar(flat(b[bb], n), flat(f[n % NL], n), THR, 1.0 / THR, ALU.min,
                                        ALU.mult).then_inc(s["ab_ready"], 1)

            def front_b(n):
                bb = n % 2
                dve.wait_ge(s["ln_ready"], n + 1)
                nc.vector.tensor_tensor(flat(lf[bb], n), flat(lf[bb], n), flat(la[bb], n),
                                        ALU.add).then_inc(s["lf_ready"], 1)

            def front_c(n):
                bb = n % 2
                dve.wait_ge(s["lf_ready"], n + 1)
                if n >= 2:
                    dve.wait_ge(s["e12_ready"], n - 1)
                nc.vector.tensor_tensor_scan(out=flat(gs[bb], n), data0=keep[tiles[n][1]][:, :],
                                             data1=flat(lf[bb], n), initial=0.0, op0=ALU.mult,
                                             op1=ALU.add).then_inc(s["g_ready"], 1)

            def take(n, i):
                r = tiles[n][1]
                p = prod0[n] + i
                lv = 7 if i == len(levels(n)) else levels(n)[i].bit_length() - 1
                dve.wait_ge(s["a_ready"], p + 1)
                if i == 0 and n >= 3:
                    dve.wait_ge(s["o_done"], n - 1)
                if p >= 1:
                    dve.wait_ge(s["a_out"], p)
                nc.vector.copy_predicated(at(n)[0:r, :, 0:r],
                                          masks[0:r, lv:lv + 1, 0:r].to_broadcast([r, H, r]).bitcast(I32),
                                          psA[p % NA][0:r, :, 0:r]).then_inc(s["a_out"], 1)

            def state_out(n):
                bb = n % 2
                dve.wait_ge(s["s_done"], n + 1)
                new, old = St[(n + 1) % 3], St[n % 3]
                if n == 3:
                    dve.wait_ge(state_stored, 16)
                if n >= 3:
                    dve.wait_ge(s["o_done"], n - 1)
                if tiles[n][2]:
                    if n >= 1:
                        dve.wait_ge(s["s_out"], n)
                    else:
                        dve.wait_ge(s["state_loaded"], 16)
                    for h in range(H):
                        last = nc.vector.scalar_tensor_tensor(
                            out=new[:, h, :], in0=old[:, h, :], scalar=heads(e1[bb], n)[:, h, tiles[n][1] - 1:tiles[n][1]],
                            in1=psS[:, h, :], op0=ALU.mult, op1=ALU.add)
                else:
                    last = nc.vector.tensor_copy(new[:, :, :], psS[:, :, :])
                last.then_inc(s["s_out"], 1)

            def out_rms(n):
                r, bb = tiles[n][1], n % 2
                dve.wait_ge(s["sq_ready"], n + 1)
                nc.vector.tensor_reduce(so[bb][0:r, :], sqo[bb][0:r, :].rearrange("p (h t) -> p h t", h=H),
                                        axis=AX.X, op=ALU.add).then_inc(s["so_ready"], 1)

            def out_scale(n):
                r, bb = tiles[n][1], n % 2
                dve.wait_ge(s["rs_ready"], n + 1)
                if n >= 2:
                    dve.wait_ge(stored[bb], 16 * (n // 2))
                nc.vector.tensor_tensor(on[bb][0:r, :].rearrange("p (h t) -> p h t", h=H), psO[bb][0:r, :, :],
                                        rs[bb][0:r, :].unsqueeze(2).to_broadcast([r, H, P]),
                                        ALU.mult).then_inc(s["osc_ready"], 1)

            def out_gate(n):
                r, bb = tiles[n][1], n % 2
                dve.wait_ge(s["osc_ready"], n + 1)
                nc.vector.tensor_tensor(on[bb][0:r, :], on[bb][0:r, :], g[n % NL][0:r, :],
                                        ALU.mult).then_inc(s["on_ready"], 1)

            front_a(0)
            front_b(0)
            front_c(0)
            for spot in SPOTS:
                if level_at(spot, 0):
                    n, i = level_at(spot, 0)
                    if i == 0:
                        dve.wait_ge(s["g_ready"], n + 1)
                    m, u = levels(n)[i], lev0[n] + i
                    if u >= NX:
                        dve.wait_ge(s["e_ready"], u - NX + 1)
                    dv, gv = blk(d[u % NX], n, m), blk(gs[n % 2], n, m)
                    nb = H * tiles[n][1] // (2 * m)
                    mid = gv[:, :, m - 1:m].to_broadcast([P, nb, m])
                    nc.vector.tensor_tensor(dv[:, :, 0:m], mid, gv[:, :, 0:m], ALU.subtract)
                    nc.vector.tensor_tensor(dv[:, :, m:2 * m], gv[:, :, m:2 * m], mid,
                                            ALU.subtract).then_inc(s["d_ready"], 1)
                if product_at(spot, TAKE):
                    take(*product_at(spot, TAKE))
                n = tile_at(spot, D2)
                if n is not None:
                    bb, r = n % 2, tiles[n][1]
                    gh = heads(gs[bb], n)
                    if n >= 2:
                        dve.wait_ge(s["e12_ready"], n - 1)
                    nc.vector.tensor_tensor(heads(d2[bb], n), gh[:, :, r - 1:r].to_broadcast([P, H, r]), gh,
                                            ALU.subtract).then_inc(s["d2_ready"], 1)
                for step, ahead, do in ((FRONT_A, 1, front_a), (FRONT_B, 1, front_b), (FRONT_C, 1, front_c),
                                        (SOUT, 0, state_out), (RMS, 0, out_rms), (OSC, 0, out_scale),
                                        (GATE, 0, out_gate)):
                    n = tile_at(spot, step)
                    if n is not None and n + ahead < N:
                        do(n + ahead)

        @block.tensor
        def _(pe):
            pe.wait_ge(s["init"], 1)
            pe.wait_ge(s["state_loaded"], 16)
            for spot in SPOTS:
                if product_at(spot, PROD):
                    n, i = product_at(spot, PROD)
                    r, p = tiles[n][1], prod0[n] + i
                    if i < len(levels(n)):
                        u = lev0[n] + i
                        pe.wait_ge(s["x_ready"], u + 1)
                        lhs = rhs = heads(x[u % NX], n)
                    else:
                        lhs, rhs = heads(k[n % NL], n), heads(q[n % NL], n)
                    if p >= NA:
                        pe.wait_ge(s["a_out"], p - NA + 1)
                    for h in range(H):
                        last = nc.tensor.matmul(psA[p % NA][0:r, h, 0:r], lhs[:, h, :], rhs[:, h, :],
                                                start=True, stop=True)
                    last.then_inc(s["a_ready"], 1)
                j = tile_at(spot, KHT)
                if j is not None:
                    bb, r = j % 2, tiles[j][1]
                    pe.wait_ge(s["qk_ready"], j + 1)
                    if j >= 1:
                        pe.wait_ge(s["khn_ready"], j)
                    for h in range(H):
                        last = nc.tensor.transpose(psK[0:r, h, :], heads(kh[bb], j)[:, h, :], ident[:, :])
                    last.then_inc(s["khT_ready"], 1)
                j = tile_at(spot, SPROD)
                if j is not None:
                    bb, r, vb = j % 2, tiles[j][1], v[j % NL]
                    pe.wait_ge(s["khn_ready"], j + 1)
                    if j >= 1:
                        pe.wait_ge(s["s_out"], j)
                    for h in range(H):
                        last = nc.tensor.matmul(psS[:, h, :], khn[bb][0:r, h * P:(h + 1) * P],
                                                vb[0:r, h * P:(h + 1) * P], start=True, stop=True)
                    last.then_inc(s["s_done"], 1)
                j = tile_at(spot, OPROD)
                if j is not None:
                    t0, r, before = tiles[j]
                    bb, vb = j % 2, v[j % NL]
                    pe.wait_ge(s["a_out"], prod0[j + 1])
                    if j >= 1:
                        pe.wait_ge(s["s_out"], j)
                    if j >= 2:
                        pe.wait_ge(s["osc_ready"], j - 1)
                    for h in range(H):
                        last = nc.tensor.matmul(psO[bb][0:r, h, :], at(j)[0:r, h, 0:r], vb[0:r, h * P:(h + 1) * P],
                                                start=True, stop=not before)
                        if before:
                            last = nc.tensor.matmul(psO[bb][0:r, h, :], heads(qh[bb], j)[:, h, :],
                                                    St[j % 3][:, h, :], start=False, stop=True)
                    last.then_inc(s["o_done"], 1)


def merge_and_ffn(nc, mix, x, w_o, norm_ffn, w_up, w_down, y):
    FP = 2
    NP = DFF // (FP * P)
    PIECE = FP * D
    NPC = KD // FP + 2 * NP
    HT = max(sum(r for _, r in th) for th in THIRDS)
    NTH = len(THIRDS)
    n0 = [sum(len(z) for z in THIRDS[:t]) for t in range(NTH)]
    ctx = ExitStack()
    with ctx:
        S = Space(nc, ctx)
        ident = S.sb("mf_ident", [P, P])
        grow = S.sb("mf_grow", [P, D])
        mhalf = S.sb("mf_mhalf", [P, 1])
        nat = [S.sb(f"mf_nat{i}", [P, D]) for i in range(2)]
        xin = [S.sb(f"mf_xin{i}", [P, D]) for i in range(2)]
        hs = [S.sb(f"mf_hs{i}", [P, D]) for i in range(2)]
        ss = S.sb("mf_ss", [P, len(TILES)])
        rstd = S.sb("mf_rstd", [P, len(TILES)])
        acc = S.sb("mf_acc", [P, max(len(z) for z in THIRDS), D])
        xhi = S.sb("mf_xhi", [P, KD, HT], F32R)
        xlo = S.sb("mf_xlo", [P, KD, HT], F32R)
        st = [S.sb(f"mf_st{i}", [P, PIECE]) for i in range(2)]
        whi = [S.sb(f"mf_whi{i}", [P, PIECE], F32R) for i in range(4)]
        wlo = [S.sb(f"mf_wlo{i}", [P, PIECE], F32R) for i in range(4)]
        uhi = S.sb("mf_uhi", [P, 2 * FP, HT], F32R)
        ulo = S.sb("mf_ulo", [P, 2 * FP, HT], F32R)
        rl = [hs[i][:, 0:HT // 2] for i in range(2)]
        sq = [hs[i][:, HT // 2:HT] for i in range(2)]
        psT = [S.ps(f"mf_psT{i}", [P, KD, P]) for i in range(2)]
        psO = [S.ps(f"mf_psO{i}", [P, D]) for i in range(2)]
        names = """init consts t_ready hi_ready lo_ready whi_ready wlo_ready o_done o_out squared mean_ready
            rstd_ready hs_ready up_done relu_ready uhi_ready sq_ready ulo_ready""".split()
        s = {z: S.sem("mf_" + z) for z in names}
        nat_loaded = [S.sem(f"mf_nat_loaded{i}") for i in range(2)]
        x_loaded = [S.sem(f"mf_x_loaded{i}") for i in range(2)]
        w_loaded = [S.sem(f"mf_w_loaded{i}") for i in range(2)]
        stored = S.sem("mf_stored")

        def t_index(t, i, second):
            return 2 * n0[t] + (len(THIRDS[t]) if second else 0) + i

        def o_index(t, i, p):
            return (NP + 1) * n0[t] + (p + 1) * len(THIRDS[t]) + i

        def up_index(t, f, b):
            return (t * DFF // P + f) * 2 + b

        def piece(t, what, p):
            k = p if what == "o" else KD // FP + 2 * p + (what == "d")
            return t * NPC + k

        def wbuf(what, p):
            return p if what == "o" else p % 2 + 2 * (what == "d")

        def piece_src(what, p):
            if what == "u":
                return w_up[:, p * FP * P:(p + 1) * FP * P].rearrange("(k p) n -> p k n", p=P)
            w = w_o if what == "o" else w_down
            return w[p * FP * P:(p + 1) * FP * P, :].rearrange("(k p) n -> p k n", p=P)

        def wait_wbuf_free(eng, t, what, p):
            if what == "o":
                if t and p < 2:
                    eng.wait_ge(s["up_done"], up_index(t, 0, 0))
                elif t:
                    eng.wait_ge(s["o_done"], o_index(t - 1, 0, p - 2 + NP - 1))
            elif p < 2:
                eng.wait_ge(s["o_done"], o_index(t, 0, 0))
            elif what == "u":
                eng.wait_ge(s["up_done"], up_index(t, FP * (p - 1), 0))
            else:
                eng.wait_ge(s["o_done"], o_index(t, 0, p - 1))

        order = [("o", p) for p in range(KD // FP)]
        for p in range(NP):
            order += [("u", p), ("d", p)]

        def split_plan(p):
            out = []
            if p + 2 < NP:
                out.append(("u", p + 2))
            if p + 1 < NP:
                out.append(("d", p + 1))
            return sorted(out, key=order.index)

        def piece_after(t, i):
            n = KD // FP
            return i if i < n - 1 else n - 1 if i == len(THIRDS[t]) - 1 else None

        block = ctx.enter_context(nc.Block())

        @block.sync
        def _(sp):
            sp.dma_start(grow[:, :], bcast_rows(norm_ffn, P)).then_inc(s["consts"], 16)

            def load_piece(t, what, p):
                m = piece(t, what, p)
                if m >= 2:
                    sp.wait_ge(s["whi_ready"], m - 1)
                    sp.wait_ge(s["wlo_ready"], m - 1)
                src = piece_src(what, p)
                sp.dma_start(st[m % 2][:, :].rearrange("p (k n) -> p k n", k=src.shape[1]), src
                             ).then_inc(w_loaded[m % 2], 16)

            def load_mixed(t, i):
                (t0, r), n = THIRDS[t][i], n0[t] + i
                if i >= 2 or t:
                    sp.wait_ge(s["t_ready"], t_index(t, i - 2, False) + 1 if i >= 2 else t_index(t, 0, False))
                sp.dma_start(nat[n % 2][0:r, :], mix[t0:t0 + r, :]).then_inc(nat_loaded[n % 2], 16)
                if piece_after(t, i) is not None:
                    load_piece(t, "o", piece_after(t, i))

            for i in range(len(THIRDS[0])):
                load_mixed(0, i)
            for t, tiles in enumerate(THIRDS):
                for i, (t0, r) in enumerate(tiles):
                    n = n0[t] + i
                    if n >= 2:
                        sp.wait_ge(s["o_out"], o_index(t, i - 2, -1) + 1 if i >= 2 else o_index(t, 0, -1))
                    sp.dma_start(xin[n % 2][0:r, :], x(t0, r)).then_inc(x_loaded[n % 2], 16)
                for what, p in order[KD // FP:]:
                    load_piece(t, what, p)
                ahead = len(THIRDS[t + 1]) if t + 1 < NTH else 0
                for i in range(min(2, ahead)):
                    load_mixed(t + 1, i)
                for i, (t0, r) in enumerate(tiles):
                    if i + 2 < ahead:
                        load_mixed(t + 1, i + 2)
                    sp.wait_ge(s["o_out"], o_index(t, i, NP - 1) + 1)
                    sp.dma_start(y(t0, r), acc[0:r, i, :]).then_inc(stored, 16)
            sp.wait_ge(stored, 16 * len(TILES))

        @block.gpsimd
        def _(pool):
            nc.gpsimd.memset(ident[:, :], 0.0).then_inc(s["init"], 1)
            nc.gpsimd.memset(mhalf[:, :], -0.5).then_inc(s["init"], 1)
            pool.wait_ge(s["init"], 2)
            nc.gpsimd.affine_select(out=ident[:, :], in_=ident[:, :], compare_op=ALU.not_equal, fill=1.0,
                                    base=0, pattern=[[-1, P]], channel_multiplier=1).then_inc(s["init"], 1)
            for n, (t0, r) in enumerate(TILES):
                pool.wait_ge(s["squared"], n + 1)
                nc.gpsimd.tensor_scalar(rstd[0:r, n:n + 1], ss[0:r, n:n + 1], 1.0 / D, EPS,
                                        ALU.mult, ALU.add).then_inc(s["mean_ready"], 1)
                pool.wait_ge(s["mean_ready"], n + 1)
                nc.gpsimd.tensor_tensor(rstd[0:r, n:n + 1], rstd[0:r, n:n + 1], mhalf[0:r, 0:1],
                                        ALU.pow).then_inc(s["rstd_ready"], 1)

        @block.scalar
        def _(act):
            def split(t, what, p):
                m = piece(t, what, p)
                act.wait_ge(w_loaded[m % 2], 16 * (m // 2 + 1))
                wait_wbuf_free(act, t, what, p)
                nc.scalar.activation(whi[wbuf(what, p)][:, :], st[m % 2][:, :], ACT.Copy
                                     ).then_inc(s["whi_ready"], 1)

            for t, tiles in enumerate(THIRDS):
                nt, base = len(tiles), tiles[0][0]
                bl = blocks_of(sum(r for _, r in tiles))

                def hi(t, i, second):
                    t0, r = THIRDS[t][i]
                    k = t_index(t, i, second)
                    act.wait_ge(s["t_ready"], k + 1)
                    if t and i == 0 and not second:
                        act.wait_ge(s["up_done"], up_index(t, 0, 0))
                    c = slice(t0 - THIRDS[t][0][0], t0 - THIRDS[t][0][0] + r)
                    nc.scalar.activation(xhi[:, :, c], psT[k % 2][:, :, 0:r], ACT.Copy).then_inc(s["hi_ready"], 1)

                def square(i):
                    n, r = n0[t] + i, tiles[i][1]
                    act.wait_ge(s["o_out"], o_index(t, i, -1) + 1)
                    if i >= 2 or t:
                        act.wait_ge(s["t_ready"], t_index(t, i - 2, True) + 1 if i >= 2 else
                                    t_index(t - 1, len(THIRDS[t - 1]) - 1, True) + 1)
                    nc.scalar.activation(hs[n % 2][0:r, :], acc[0:r, i, :], ACT.Square,
                                         accum_out=ss[0:r, n:n + 1]).then_inc(s["squared"], 1)

                def hi_mixed(t):
                    for i in range(len(THIRDS[t])):
                        hi(t, i, False)
                        if piece_after(t, i) is not None:
                            split(t, "o", piece_after(t, i))

                if t == 0:
                    hi_mixed(0)
                for i in range(nt):
                    square(i)
                    if i >= 1:
                        hi(t, i - 1, True)
                hi(t, nt - 1, True)
                split(t, "u", 0)
                for p in range(-1, NP):
                    for what, pp in split_plan(p):
                        split(t, what, pp)
                    if p + 1 < NP:
                        for f in range(FP * (p + 1), FP * (p + 2)):
                            for b, (c0, cn) in enumerate(bl):
                                k = up_index(t, f, b)
                                ps = psT[(k % 4) // 2][:, :, :].rearrange("p k n -> p (k n)")[
                                    :, (k % 2) * 512:(k % 2) * 512 + cn]
                                act.wait_ge(s["up_done"], k + 1)
                                if k >= 2:
                                    act.wait_ge(s["sq_ready"], k - 1)
                                nc.scalar.activation(rl[k % 2][:, 0:cn], ps, ACT.Relu).then_inc(s["relu_ready"], 1)
                                act.wait_ge(s["relu_ready"], k + 1)
                                if b == 0 and p >= 1:
                                    act.wait_ge(s["o_done"], o_index(t, 0, p))
                                nc.scalar.activation(uhi[:, f % (2 * FP), c0:c0 + cn], rl[k % 2][:, 0:cn],
                                                     ACT.Square).then_inc(s["uhi_ready"], 1)
                if t + 1 < NTH:
                    hi_mixed(t + 1)

        @block.vector
        def _(dve):
            def split(t, what, p):
                m = piece(t, what, p)
                dve.wait_ge(s["whi_ready"], m + 1)
                wait_wbuf_free(dve, t, what, p)
                b = wbuf(what, p)
                nc.vector.tensor_tensor(wlo[b][:, :], st[m % 2][:, :], whi[b][:, :].bitcast(F32),
                                        ALU.subtract).then_inc(s["wlo_ready"], 1)

            dve.wait_ge(s["consts"], 16)
            for t, tiles in enumerate(THIRDS):
                nt, base = len(tiles), tiles[0][0]
                bl = blocks_of(sum(r for _, r in tiles))

                def lo(t, i, second):
                    t0, r = THIRDS[t][i]
                    k = t_index(t, i, second)
                    dve.wait_ge(s["hi_ready"], k + 1)
                    c = slice(t0 - THIRDS[t][0][0], t0 - THIRDS[t][0][0] + r)
                    nc.vector.tensor_tensor(xlo[:, :, c], psT[k % 2][:, :, 0:r], xhi[:, :, c].bitcast(F32),
                                            ALU.subtract).then_inc(s["lo_ready"], 1)

                def add_x(i):
                    n, r, k = n0[t] + i, tiles[i][1], o_index(t, i, -1)
                    dve.wait_ge(s["o_done"], k + 1)
                    dve.wait_ge(x_loaded[n % 2], 16 * (n // 2 + 1))
                    if t:
                        dve.wait_ge(stored, 16 * n0[t])
                    nc.vector.tensor_tensor(acc[0:r, i, :], psO[k % 2][0:r, :], xin[n % 2][0:r, :],
                                            ALU.add).then_inc(s["o_out"], 1)

                def scale(i):
                    n, r = n0[t] + i, tiles[i][1]
                    dve.wait_ge(s["rstd_ready"], n + 1)
                    nc.vector.scalar_tensor_tensor(out=hs[n % 2][0:r, :], in0=acc[0:r, i, :],
                                                   scalar=rstd[0:r, n:n + 1], in1=grow[0:r, :],
                                                   op0=ALU.mult, op1=ALU.mult).then_inc(s["hs_ready"], 1)

                def lo_mixed(t, i):
                    lo(t, i, False)
                    if piece_after(t, i) is not None:
                        split(t, "o", piece_after(t, i))

                for i in range(nt if t == 0 else 0):
                    lo_mixed(0, i)
                for i in range(nt):
                    add_x(i)
                    scale(i)
                    if i >= 1:
                        lo(t, i - 1, True)
                lo(t, nt - 1, True)
                split(t, "u", 0)
                for p in range(-1, NP):
                    for what, pp in split_plan(p):
                        split(t, what, pp)
                    if p + 1 < NP:
                        for f in range(FP * (p + 1), FP * (p + 2)):
                            for b, (c0, cn) in enumerate(bl):
                                k = up_index(t, f, b)
                                ps = psT[(k % 4) // 2][:, :, :].rearrange("p k n -> p (k n)")[
                                    :, (k % 2) * 512:(k % 2) * 512 + cn]
                                dve.wait_ge(s["relu_ready"], k + 1)
                                nc.vector.tensor_tensor(sq[k % 2][:, 0:cn], ps, rl[k % 2][:, 0:cn],
                                                        ALU.mult).then_inc(s["sq_ready"], 1)
                                dve.wait_ge(s["sq_ready"], k + 1)
                                dve.wait_ge(s["uhi_ready"], k + 1)
                                nc.vector.tensor_tensor(ulo[:, f % (2 * FP), c0:c0 + cn], sq[k % 2][:, 0:cn],
                                                        uhi[:, f % (2 * FP), c0:c0 + cn].bitcast(F32),
                                                        ALU.subtract).then_inc(s["ulo_ready"], 1)
                    if p >= 0:
                        for i, (t0, r) in enumerate(tiles):
                            k = o_index(t, i, p)
                            dve.wait_ge(s["o_done"], k + 1)
                            dve.wait_ge(s["o_out"], k)
                            nc.vector.tensor_tensor(acc[0:r, i, :], psO[k % 2][0:r, :], acc[0:r, i, :],
                                                    ALU.add).then_inc(s["o_out"], 1)
                            if p == NP - 1 and t + 1 < NTH and i + 1 < len(THIRDS[t + 1]):
                                lo_mixed(t + 1, i)
                if t + 1 < NTH:
                    for i in range(min(nt, len(THIRDS[t + 1]) - 1), len(THIRDS[t + 1])):
                        lo_mixed(t + 1, i)

        @block.tensor
        def _(pe):
            pe.wait_ge(s["init"], 3)
            for t, tiles in enumerate(THIRDS):
                nt, base = len(tiles), tiles[0][0]
                bl = blocks_of(sum(r for _, r in tiles))

                def turn(t, i, second):
                    t0, r = THIRDS[t][i]
                    n, k = n0[t] + i, t_index(t, i, second)
                    if second:
                        pe.wait_ge(s["hs_ready"], n + 1)
                    else:
                        pe.wait_ge(nat_loaded[n % 2], 16 * (n // 2 + 1))
                    if k >= 2:
                        pe.wait_ge(s["lo_ready"], k - 1)
                    if t and i == 0 and not second:
                        pe.wait_ge(s["sq_ready"], up_index(t, 0, 0))
                    src = (hs if second else nat)[n % 2]
                    for j in range(KD):
                        last = nc.tensor.transpose(psT[k % 2][:, j, 0:r], src[0:r, j * P:(j + 1) * P],
                                                   ident[0:r, 0:r])
                    last.then_inc(s["t_ready"], 1)

                def product(k, r, steps, parts_ready={}):
                    if k >= 2:
                        pe.wait_ge(s["o_out"], k - 1)
                    for half in range(2):
                        c = slice(half * 512, half * 512 + 512)
                        for j, (xa, wa) in enumerate(steps):
                            if half == 0 and j in parts_ready:
                                pe.wait_ge(s["wlo_ready"], parts_ready[j])
                            last = nc.tensor.matmul(psO[k % 2][0:r, c], xa, wa[:, c], start=j == 0,
                                                    stop=j == len(steps) - 1)
                    last.then_inc(s["o_done"], 1)

                def out_proj(i):
                    t0, r = tiles[i]
                    c = slice(t0 - base, t0 - base + r)
                    steps = []
                    for j in range(KD):
                        b, w0 = j // FP, (j % FP) * D
                        for xa, wa in ((xhi, whi), (xhi, wlo), (xlo, whi)):
                            steps.append((xa[:, j, c], wa[b][:, w0:w0 + D]))
                    ready = {3 * FP * q: piece(t, "o", q) + 1 for q in range(KD // FP)} if i == 0 else {}
                    product(o_index(t, i, -1), r, steps, ready)

                for i in range(nt if t == 0 else 0):
                    turn(0, i, False)
                for i in range(nt):
                    pe.wait_ge(s["lo_ready"], t_index(t, i, False) + 1)
                    out_proj(i)
                    if i >= 1:
                        turn(t, i - 1, True)
                turn(t, nt - 1, True)
                pe.wait_ge(s["lo_ready"], t_index(t, nt - 1, True) + 1)
                for p in range(-1, NP):
                    if p + 1 < NP:
                        pe.wait_ge(s["wlo_ready"], piece(t, "u", p + 1) + 1)
                        b4 = wbuf("u", p + 1)
                        for f in range(FP * (p + 1), FP * (p + 2)):
                            for b, (c0, cn) in enumerate(bl):
                                k = up_index(t, f, b)
                                ps = psT[(k % 4) // 2][:, :, :].rearrange("p k n -> p (k n)")[
                                    :, (k % 2) * 512:(k % 2) * 512 + cn]
                                if k >= 4:
                                    pe.wait_ge(s["sq_ready"], k - 3)
                                for j in range(KD):
                                    w0 = j * FP * P + (f % FP) * P
                                    for q, (wa, xa) in enumerate(((whi, xhi), (whi, xlo), (wlo, xhi))):
                                        last = nc.tensor.matmul(ps, wa[b4][:, w0:w0 + P], xa[:, j, c0:c0 + cn],
                                                                start=j == 0 and q == 0,
                                                                stop=j == KD - 1 and q == 2)
                                last.then_inc(s["up_done"], 1)
                    if p >= 0:
                        pe.wait_ge(s["wlo_ready"], piece(t, "d", p) + 1)
                        pe.wait_ge(s["ulo_ready"], up_index(t, FP * (p + 1), 0))
                        bd = wbuf("d", p)
                        for i, (t0, r) in enumerate(tiles):
                            c = slice(t0 - base, t0 - base + r)
                            steps = []
                            for j in range(FP):
                                f = (FP * p + j) % (2 * FP)
                                for ua, wa in ((uhi, whi), (uhi, wlo), (ulo, whi)):
                                    steps.append((ua[:, f, c], wa[bd][:, j * D:(j + 1) * D]))
                            product(o_index(t, i, p), r, steps)
                            if p == NP - 1 and t + 1 < NTH and i < len(THIRDS[t + 1]):
                                turn(t + 1, i, False)
                if t + 1 < NTH:
                    for i in range(nt, len(THIRDS[t + 1])):
                        turn(t + 1, i, False)


def build(nc, a, outs):
    (yp, ys, akp, avp, bkp, bvp, csp, aks, avs, bks, bvs, css) = outs

    def rows(ap):
        return ap[0, 0].rearrange("t h d -> t (h d)")

    proj = nc.dram_tensor("scratch_proj", [NG, T, G], F32).ap()
    tr = nc.dram_tensor("scratch_tr", [3, H, P, T], F32).ap()
    mix = nc.dram_tensor("scratch_mix", [T, D], F32).ap()
    line = nc.dram_tensor("scratch_line", [H, NLINE], F32).ap()

    def x(t0, r):
        return a["x_prompt"][0, t0:t0 + r, :] if t0 < SEQ else a["x_sample"][0, 0:r, :]

    def y(t0, r):
        return yp[0, t0:t0 + r, :] if t0 < SEQ else ys[0, 0:r, :]

    gains = [a[n][0] for n in ("qnorm_a", "knorm_a", "qnorm_b", "knorm_b")]
    natural = {"akp": akp, "avp": avp, "bkp": bkp, "bvp": bvp, "aks": aks, "avs": avs, "bks": bks, "bvs": bvs}
    project(nc, x, a["norm_mix"][0], a["w_in"][0], gains, a["lower_bounds"][0],
            a["onorm_c"][0], proj, tr, {n: rows(z) for n, z in natural.items()})

    def source(group, col, cache=None):
        def at(seq, t0, r):
            if seq == "s" and t0 < PAST:
                return rows(cache)[t0:t0 + r, :]
            t = SEQ if seq == "s" else t0
            return proj[group, t:t + r, col:col + WH]
        return at

    def by_head(at):
        return lambda seq, t0, r: at(seq, t0, r).rearrange("t (h d) -> t h d", h=H)

    attend(nc, "A", by_head(source(QKA, 0)), by_head(source(QKA, WH, a["cache_a_k"])),
           source(VQ, 0, a["cache_a_v"]), None, mix[:, 0:WH])
    attend(nc, "B", by_head(source(VQ, WH)), by_head(source(KV, 0, a["cache_b_k"])),
           source(KV, WH, a["cache_b_v"]), (a["rel_bias_b"][0], line), mix[:, WH:2 * WH])
    recur(nc, tr, lambda t0, r: proj[IC, t0:t0 + r, :], lambda t0, r: proj[GC, t0:t0 + r, :],
          a["state_c"][0, 0], [csp[0, 0], css[0, 0]], mix[:, 2 * WH:D])
    merge_and_ffn(nc, mix, x, a["w_o"][0], a["norm_ffn"][0], a["w_up"][0], a["w_down"][0], y)


_INS = ["x_prompt", "x_sample", "cache_a_k", "cache_a_v", "cache_b_k", "cache_b_v", "state_c", "norm_mix", "w_in",
        "qnorm_a", "knorm_a", "qnorm_b", "knorm_b", "rel_bias_b", "lower_bounds", "onorm_c", "w_o", "norm_ffn",
        "w_up", "w_down"]
_KP, _KB, _KS = (1, 1, SEQ, H, DH), (1, 1, PREV * CHUNK, H, DH), (1, 1, NEW, H, DH)
_ST = (1, 1, H, P, P)
_OUTS = [(1, SEQ, D), (1, NEW, D), _KP, _KP, _KB, _KB, _ST, _KS, _KS, _KS, _KS, _ST]


def kernel(**inputs):
    import numpy as np
    import concourse.bacc as bacc
    from concourse.bass_utils import run_bass_kernel_spmd

    nc = bacc.Bacc("TRN2", target_bir_lowering=False, num_devices=1)
    arrays, a = {}, {}
    for name in _INS:
        v = np.ascontiguousarray(inputs[name])
        arrays["in_" + name] = v
        a[name] = nc.dram_tensor("in_" + name, v.shape, mybir.dt.from_np(v.dtype), kind="ExternalInput").ap()
    outs = [nc.dram_tensor(f"out_{i}", shape, F32, kind="ExternalOutput").ap() for i, shape in enumerate(_OUTS)]
    build(nc, a, outs)
    r = run_bass_kernel_spmd(nc, [arrays], core_ids=[0])
    return tuple(r.results[0][f"out_{i}"] for i in range(len(_OUTS)))
```
